# Optimizing a Trainium2 kernel written in Bass

```python
import jax, jax.numpy as jnp
from jax import lax
import numpy as np

D_MODEL = 1024
BATCH = 1
SEQ = 2048
DEPTH = 1
DEC_BATCH = 1
DEC_SEQ = 64
PAST_LEN = 1024

CHUNK = 64
N_BRANCH = 4
W_BR = D_MODEL // 2
GMLP_CHUNK = 128
GMLP_HEADS = 4
GMLP_HD = W_BR // GMLP_HEADS
CONV_K = 31
POOL_WINDOWS = (2, 4, 8, 16)
POOL_GROUPS = len(POOL_WINDOWS)
POOL_GD = W_BR // POOL_GROUPS
POOL_STATE = max(POOL_WINDOWS) - 1
SHORT_K = 3
N_PARTS = 12
N_IN = N_PARTS * W_BR + N_BRANCH * D_MODEL
SPLITS = tuple(W_BR * i for i in range(1, N_PARTS + 1))
EPS = 1e-6

kernel_name = 'hybrid_gated_branch_streaming_step'

def rmsnorm(x, g):
    xf = x.astype(jnp.float32)
    r = lax.rsqrt(jnp.mean(xf * xf, axis=-1, keepdims=True) + EPS)
    return (xf * r).astype(x.dtype) * g

def layernorm(x, g, b):
    xf = x.astype(jnp.float32)
    mu = jnp.mean(xf, axis=-1, keepdims=True)
    var = jnp.mean(jnp.square(xf - mu), axis=-1, keepdims=True)
    return ((xf - mu) * lax.rsqrt(var + EPS)).astype(x.dtype) * g + b

def causal_depthwise(ext, w):
    c = ext.shape[-1]
    return lax.conv_general_dilated(ext, w[:, None, :].astype(ext.dtype), window_strides=(1,),
                                    padding='VALID', dimension_numbers=('NWC', 'WIO', 'NWC'),
                                    feature_group_count=c)

def gmlp_spatial(u, v, w_s, b_s):
    bsz, t, _ = v.shape
    ln = min(t, GMLP_CHUNK)
    n = t // ln
    mask = jnp.tril(jnp.ones((ln, ln), v.dtype))
    w = w_s[:, :ln, :ln] * mask
    vc = v.reshape(bsz, n, ln, GMLP_HEADS, GMLP_HD)
    mixed = jnp.einsum('hts,bnshc->bnthc', w, vc) + b_s[:, :ln].T[None, None, :, :, None]
    return u * mixed.reshape(bsz, t, W_BR)

def multiscale_pool(ext, start_pos, pool_w, pool_scale):
    bsz = ext.shape[0]
    t = ext.shape[1] - POOL_STATE
    xf = ext.astype(jnp.float32)
    cs = jnp.concatenate([jnp.zeros_like(xf[:, :1]), jnp.cumsum(xf, axis=1)], axis=1)
    pos = start_pos + jnp.arange(t)
    x_tok = xf[:, POOL_STATE:]
    outs = []
    for g, w in enumerate(POOL_WINDOWS):
        sl = slice(g * POOL_GD, (g + 1) * POOL_GD)
        hi = cs[:, POOL_STATE + 1:, sl]
        lo = cs[:, POOL_STATE + 1 - w:POOL_STATE + 1 - w + t, sl]
        cnt = jnp.minimum(pos + 1, w).astype(jnp.float32)[None, :, None]
        outs.append((hi - lo) / cnt - x_tok[:, :, sl])
    p = jnp.stack(outs, axis=2).astype(ext.dtype)
    p = jnp.einsum('btgc,gcd->btgd', p, pool_w).reshape(bsz, t, W_BR)
    return p * pool_scale

def trunk(x, conv_states, pool_states, short_states, start_pos, g_pre, g_post, w_in, b_gate,
          ln_v_g, ln_v_b, w_s, b_s, conv_b_w, conv_b_bias, ln_b_g, ln_b_b, pool_w, pool_scale,
          conv_d_w, w_branch, w_out):
    bsz, t, _ = x.shape
    new_conv, new_pool, new_short, v_rows = [], [], [], []
    for l in range(DEPTH):
        h = rmsnorm(x, g_pre[l])
        proj = h @ w_in[l]
        (a_u, a_v, a_z, b_a, b_b, b_z, c_x, c_z, d_b, d_c, d_x, d_z,
         gate_logits) = jnp.split(proj, SPLITS, axis=-1)
        v_n = layernorm(a_v, ln_v_g[l], ln_v_b[l])
        out_a = gmlp_spatial(a_u, v_n, w_s[l], b_s[l]) * jax.nn.silu(a_z)
        glu = b_a * jax.nn.sigmoid(b_b)
        ext_b = jnp.concatenate([conv_states[l], glu], axis=1)
        cb = causal_depthwise(ext_b, conv_b_w[l]) + conv_b_bias[l]
        out_b = jax.nn.silu(layernorm(cb, ln_b_g[l], ln_b_b[l])) * jax.nn.silu(b_z)
        ext_c = jnp.concatenate([pool_states[l], c_x], axis=1)
        out_c = multiscale_pool(ext_c, start_pos, pool_w[l], pool_scale[l]) * jax.nn.silu(c_z)
        ext_d = jnp.concatenate([short_states[l], d_c * d_x], axis=1)
        out_d = d_b * causal_depthwise(ext_d, conv_d_w[l]) * jax.nn.silu(d_z)
        gates = jax.nn.sigmoid(gate_logits + b_gate[l]).reshape(bsz, t, N_BRANCH, D_MODEL)
        merged = gates[:, :, 0] * (out_a @ w_branch[l, 0])
        merged = merged + gates[:, :, 1] * (out_b @ w_branch[l, 1])
        merged = merged + gates[:, :, 2] * (out_c @ w_branch[l, 2])
        merged = merged + gates[:, :, 3] * (out_d @ w_branch[l, 3])
        y = merged @ w_out[l]
        x = x + rmsnorm(y, g_post[l])
        new_conv.append(ext_b[:, -(CONV_K - 1):])
        new_pool.append(ext_c[:, -POOL_STATE:])
        new_short.append(ext_d[:, -(SHORT_K - 1):])
        v_rows.append(v_n)
    return x, jnp.stack(new_conv), jnp.stack(new_pool), jnp.stack(new_short), jnp.stack(v_rows)

def setup_inputs(seed: int = 0) -> dict:
    key = jax.random.key(seed)
    ks = jax.random.split(key, 22)
    n = jax.random.normal
    f32 = jnp.float32
    return {
        'x_prompt': n(ks[0], (BATCH, SEQ, D_MODEL), f32),
        'x_sample': n(ks[1], (DEC_BATCH, DEC_SEQ, D_MODEL), f32),
        'state_conformer_conv': 0.5 * n(ks[2], (DEPTH, DEC_BATCH, CONV_K - 1, W_BR), f32),
        'state_pool': n(ks[3], (DEPTH, DEC_BATCH, POOL_STATE, W_BR), f32),
        'state_short_conv': 0.5 * n(ks[4], (DEPTH, DEC_BATCH, SHORT_K - 1, W_BR), f32),
        'g_pre': 1.0 + 0.05 * n(ks[5], (DEPTH, D_MODEL), f32),
        'g_post': 1.0 + 0.05 * n(ks[6], (DEPTH, D_MODEL), f32),
        'w_in': n(ks[7], (DEPTH, D_MODEL, N_IN), f32) * D_MODEL ** -0.5,
        'b_gate': 0.02 * n(ks[8], (DEPTH, N_BRANCH * D_MODEL), f32),
        'ln_v_g': 1.0 + 0.05 * n(ks[9], (DEPTH, W_BR), f32),
        'ln_v_b': 0.02 * n(ks[10], (DEPTH, W_BR), f32),
        'w_s': n(ks[11], (DEPTH, GMLP_HEADS, GMLP_CHUNK, GMLP_CHUNK), f32) * GMLP_CHUNK ** -0.5,
        'b_s': 1.0 + 0.1 * n(ks[12], (DEPTH, GMLP_HEADS, GMLP_CHUNK), f32),
        'conv_b_w': n(ks[13], (DEPTH, CONV_K, W_BR), f32) * CONV_K ** -0.5,
        'conv_b_bias': 0.02 * n(ks[14], (DEPTH, W_BR), f32),
        'ln_b_g': 1.0 + 0.05 * n(ks[15], (DEPTH, W_BR), f32),
        'ln_b_b': 0.02 * n(ks[16], (DEPTH, W_BR), f32),
        'pool_w': n(ks[17], (DEPTH, POOL_GROUPS, POOL_GD, POOL_GD), f32) * POOL_GD ** -0.5,
        'pool_scale': 1.0 + 0.1 * n(ks[18], (DEPTH, W_BR), f32),
        'conv_d_w': n(ks[19], (DEPTH, SHORT_K, W_BR), f32) * SHORT_K ** -0.5,
        'w_branch': n(ks[20], (DEPTH, N_BRANCH, W_BR, D_MODEL), f32) * W_BR ** -0.5,
        'w_out': n(ks[21], (DEPTH, D_MODEL, D_MODEL), f32) * D_MODEL ** -0.5,
    }

def reference(x_prompt, x_sample, state_conformer_conv, state_pool, state_short_conv, g_pre, g_post,
              w_in, b_gate, ln_v_g, ln_v_b, w_s, b_s, conv_b_w, conv_b_bias, ln_b_g, ln_b_b,
              pool_w, pool_scale, conv_d_w, w_branch, w_out):
    assert x_sample.shape[1] <= CHUNK
    weights = (g_pre, g_post, w_in, b_gate, ln_v_g, ln_v_b, w_s, b_s, conv_b_w, conv_b_bias,
               ln_b_g, ln_b_b, pool_w, pool_scale, conv_d_w, w_branch, w_out)
    bp = x_prompt.shape[0]
    dt = x_prompt.dtype
    zc = jnp.zeros((DEPTH, bp, CONV_K - 1, W_BR), dt)
    zp = jnp.zeros((DEPTH, bp, POOL_STATE, W_BR), dt)
    zs = jnp.zeros((DEPTH, bp, SHORT_K - 1, W_BR), dt)
    y_prompt, conv_p, pool_p, short_p, _ = trunk(x_prompt, zc, zp, zs, 0, *weights)
    y_sample, conv_s, pool_s, short_s, v_s = trunk(x_sample, state_conformer_conv, state_pool,
                                                   state_short_conv, PAST_LEN, *weights)
    return (y_prompt, y_sample, conv_p, pool_p, short_p, conv_s, pool_s, short_s, v_s)


_drawn_inputs = setup_inputs


def setup_inputs(seed=0):
    import zlib

    import numpy as np

    out = dict(_drawn_inputs(seed))
    spreads = {}
    factors = {'state_short_conv': 8.768,
     'b_gate': 8.0,
     'ln_v_b': 2.725,
     'conv_b_bias': 6.788,
     'ln_b_g': 3.954,
     'ln_b_b': 23.286,
     'state_pool': 3.302,
     'pool_scale': 3.015,
     'b_s': 3.374}
    for name, (base, spread) in spreads.items():
        noise = np.random.default_rng([zlib.crc32(name.encode()), seed]).standard_normal(out[name].shape)
        drawn = base * np.exp(spread * noise) if base else spread * noise
        out[name] = __import__('jax').numpy.asarray(drawn.astype(out[name].dtype))
    for name, factor in factors.items():
        out[name] = (out[name] * factor).astype(out[name].dtype)
    return out
```

```python
import concourse.bass as bass
from concourse import mybir

F32 = mybir.dt.float32
F32R = mybir.dt.float32r
ALU = mybir.AluOpType
ACT = mybir.ActivationFunctionType

P = 128
DM = 1024
WB = 512
SEQ = 2048
DEC = 64
KT = DM // P
CT = WB // P
CK = 31
CH = CK - 1
PH = 15
SH = 2
EPS = 1e-6
BLK = 512
NBLK = SEQ // BLK
WMAX = BLK + DEC
RING = 4
AHEAD = RING - 1

SECTIONS = [("B", 8), ("V", 4), ("C", 8), ("M", 8), ("G0", 16), ("D", 16), ("G1", 16), ("Z", 4),
            ("G2", 16), ("G3", 16), ("O", 8)]
UNIT0, MAIN0 = {}, {}
_u = _m = 0
for _n, _c in SECTIONS:
    UNIT0[_n], MAIN0[_n] = _u, _m
    _u += _c
    _m += _c // 2 if _n[0] == "G" else _c
UPB, MAIN = _u, _m
NU = UPB * NBLK
A_U, A_V, A_Z, B_A, B_B, B_Z, C_X, C_Z, D_B, D_C, D_X, D_Z = range(12)
BRANCHES = [2, 0, 3, 1]
OUTBUF = [0, 1, 0, 1]
COLS = {}
_o = 0
for _n, _c in [("b_gate", 4 * KT), ("conv_w", CT * CK), ("conv_bias", CT), ("ln_g", CT), ("ln_b", CT),
               ("pool_scale", CT), ("short_w", CT * 3), ("g_pre", KT), ("inv_count", 16)]:
    COLS[_n] = _o
    _o += _c
NCOLS = _o
ROWS = DM + 2 * WB


def half_unit(u):
    r = u % UPB
    return any(n[0] == "G" and UNIT0[n] <= r < UNIT0[n] + c and (r - UNIT0[n]) % 2 for n, c in SECTIONS)


def unit_tiles(u):
    return CT if half_unit(u) else KT


def side_jobs():
    first, k = {}, 0
    first["H", 0] = k
    k += BLK // P
    for j in range(NBLK):
        last = j == NBLK - 1
        for name, n in [("Y", BLK // P if j else 0), ("V", 3 if last else 2), ("P", CT), ("M", CT), ("L", 2)]:
            first[name, j] = k
            k += n
        if not last:
            first["H", j + 1] = k
            k += BLK // P + (1 if j + 1 == NBLK - 1 else 0)
    first["Y", NBLK] = k
    return first


SIDE = side_jobs()


def build(nc, x_prompt, x_sample, w_main, w_branch, cols, rows, bs_rows, ws_t, mask_t, pool_w, ident_in,
          st_conv, st_pool, st_short, y_prompt, y_sample, conv_p, pool_p, short_p, conv_s, pool_s,
          short_s, v_s):
    at = [0]

    def sb(name, shape, dt=F32, addr=None):
        n = 4
        for s in shape[1:]:
            n *= s
        if addr is None:
            addr = at[0]
            at[0] += (n + 31) // 32 * 32
        return nc.alloc_sbuf_tensor_at(name, list(shape), dt, offset=addr).ap()

    at[0] = (nc.sbuf_base + 31) // 32 * 32
    h_hi, h_lo = sb("h_hi", [P, KT, WMAX], F32R), sb("h_lo", [P, KT, WMAX], F32R)
    out_hi = [sb(f"out_hi{b}", [P, CT, WMAX], F32R) for b in range(2)]
    out_lo = [sb(f"out_lo{b}", [P, CT, WMAX], F32R) for b in range(2)]
    w_raw = [sb(f"w_raw{s}", [P, DM]) for s in range(RING)]
    w_hi = [sb(f"w_hi{s}", [P, DM], F32R) for s in range(RING)]
    w_lo = [sb(f"w_lo{s}", [P, DM], F32R) for s in range(RING)]
    GL = CH + BLK + CH + DEC
    glu = sb("glu", [P, CT, GL])
    cb = sb("cb", [P, CT, WMAX])
    EL = PH + BLK + PH + DEC + 2
    a = at[0]
    merged = sb("merged", [P, KT, WMAX])
    yT = sb("yT", [P, KT, WMAX], addr=a)
    vT = sb("vT", [P, CT, WMAX], addr=a)
    a += CT * WMAX * 4
    win_a = sb("win_a", [P, EL], addr=a)
    pooled = [sb(f"pooled{b}", [P, WMAX], addr=a + EL * 4 + b * WMAX * 4) for b in range(2)]
    a = at[0]
    v_n = sb("v_n", [P, BLK // P + 1, WB])
    xres = [sb(f"xres{b}", [P, DM], addr=a + b * DM * 4) for b in range(2)]
    a = at[0]
    xt = [sb(f"xt{b}", [P, DM]) for b in range(2)]
    cpy = [sb(f"cpy{b}", [P, WMAX], addr=a + b * WMAX * 4) for b in range(2)]
    win_b = sb("win_b", [P, EL], addr=a + 2 * WMAX * 4)
    sig = [sb(f"sig{b}", [P, WMAX]) for b in range(2)]
    a = at[0]
    ext = [sb(f"ext{b}", [P, EL]) for b in range(2)]
    ynorm = sb("ynorm", [P, DM], addr=a)
    tmp = sb("tmp", [P, WMAX])
    g_post_bc = sb("g_post_bc", [P, DM])
    lnv_g_bc, lnv_b_bc = sb("lnv_g_bc", [P, WB]), sb("lnv_b_bc", [P, WB])
    bs_bc = sb("bs_bc", [P, CT, P])
    ws = sb("ws", [P, CT, P])
    poolw = sb("poolw", [P, CT, P])
    ident = sb("ident", [P, P])
    mean_mat = sb("mean_mat", [P, P])
    col = sb("col", [P, NCOLS])
    halo_g, halo_c, halo_d = (sb(f"halo_{n}", [P, CT, w]) for n, w in (("g", CH), ("c", PH), ("d", SH)))
    smp_g, smp_c, smp_d = (sb(f"smp_{n}", [P, CT, w]) for n, w in (("g", CH), ("c", PH), ("d", SH)))
    stats = sb("stats", [P, 8, 6])
    mv = sb("mv", [P, 8, 2])
    msq = sb("msq", [P, 8])
    rstd = sb("rstd", [P, 8])
    nhalf = sb("nhalf", [P, 8])
    assert at[0] <= nc.sbuf_usable_end, (at[0], nc.sbuf_usable_end)
    acc = nc.alloc_psum_tensor("acc", [P, 2, 2, 512], F32).ap()
    side = nc.alloc_psum_tensor("side", [P, 2, 1024], F32).ap()

    sem = nc.alloc_semaphore
    w_landed = [sem(f"w_landed{s}") for s in range(RING)]
    w_hi_done, w_lo_done = sem("w_hi_done"), sem("w_lo_done")
    const_loaded, const_ready, halo_zeroed = sem("const_loaded"), sem("const_ready"), sem("halo_zeroed")
    acc_done = sem("acc_done")
    acc_free = [sem(f"acc_free{s}") for s in range(2)]
    side_done, side_free = sem("side_done"), sem("side_free")
    z_sig_ready, sig_used = sem("z_sig_ready"), sem("sig_used")
    cpy_used, ext_used = sem("cpy_used"), sem("ext_used")
    vn_ready, pooled_ready, sums_ready = sem("vn_ready"), sem("pooled_ready"), sem("sums_ready")
    res_ready, merge_ready, h_ready, xs_ready = sem("res_ready"), sem("merge_ready"), sem("h_ready"), sem("xs_ready")
    msq_ready, rstd_ready = sem("msq_ready"), sem("rstd_ready")
    var_ready, std_ready, ln_ready, lnsig_ready = sem("var_ready"), sem("std_ready"), sem("ln_ready"), sem("lnsig_ready")
    x_loaded = [sem(f"x_loaded{b}") for b in range(2)]
    xres_loaded = [sem(f"xres_loaded{b}") for b in range(2)]
    y_ready = sem("y_ready")
    y_stored = [sem(f"y_stored{b}") for b in range(2)]
    states_ready, states_stored, v_stored = sem("states_ready"), sem("states_stored"), sem("v_stored")

    def width(j):
        return WMAX if j == NBLK - 1 else BLK

    def tiles(j):
        return [(0, WMAX // 2), (WMAX // 2, WMAX // 2)] if j == NBLK - 1 else [(0, BLK)]

    def n_tok(j):
        return BLK // P + (1 if j == NBLK - 1 else 0)

    def rows_of(t):
        return DEC if t == BLK // P else P

    def accv(s, j):
        if j == NBLK - 1:
            return acc[:, s, :, 0:WMAX // 2]
        return acc[:, s, 0, :]

    def tv(ap, j):
        if j == NBLK - 1:
            return ap[:, 0:WMAX].rearrange("p (a b) -> p a b", a=2)
        return ap[:, 0:BLK]

    def segments(j, hist):
        s = [(0, BLK, hist)]
        return s + [(BLK, DEC, BLK + 2 * hist)] if j == NBLK - 1 else s

    def pieces(j, hist):
        out = []
        for t0, n, c0 in segments(j, hist):
            for b, (a0, m) in enumerate(tiles(j)):
                lo, hi = max(t0, a0), min(t0 + n, a0 + m)
                if lo < hi:
                    out.append((lo, hi - lo, c0 + lo - t0, b, lo - a0))
        return out

    def side_pieces(j):
        return [(0, BLK), (BLK, DEC)] if j == NBLK - 1 else [(0, BLK)]

    def c1(name, i=0):
        return col[:, bass.ds(COLS[name] + i, 1)]

    def f(ap):
        return ap.bitcast(F32)

    def x_rows(j, t):
        return x_sample[:, :] if t == BLK // P else x_prompt[j * BLK + t * P:j * BLK + (t + 1) * P, :]

    def y_rows(j, t):
        return y_sample[:, :] if t == BLK // P else y_prompt[j * BLK + t * P:j * BLK + (t + 1) * P, :]

    TPB = BLK // P

    def xn(j, t):
        return j * TPB + t

    def each(eng, start, end, body):
        if end - start == 1:
            body(start)
        else:
            with eng.Fori(start, end) as i:
                body(i)

    block = nc.Block()
    blk = block.__enter__()

    @blk.sync
    def _(sp):
        def load(u, r, src, n):
            if not isinstance(u, int) or u >= RING:
                sp.wait_ge(w_lo_done, u - RING + 1)
            sp.dma_start(w_raw[r % RING][:, 0:n], src).then_inc(w_landed[r % RING], 16)

        for j in range(NBLK):
            for g, (name, count) in enumerate(SECTIONS):
                u0 = j * UPB + UNIT0[name]
                if name[0] == "G":
                    ph = int(name[1])

                    def body(i):
                        for r in range(4):
                            m = i * 2 + r // 2
                            if r % 2 == 0:
                                src = w_main[bass.ds(MAIN0[name] + m, 1), :, :].rearrange("o p n -> (o p) n")
                                load(u0 + i * 4 + r, r, src, DM)
                            else:
                                src = w_branch[bass.ds(ph * KT + m, 1), :, :].rearrange("o p n -> (o p) n")
                                load(u0 + i * 4 + r, r, src, WB)
                    each(sp, 0, count // 4, body)
                else:
                    def body(i):
                        for r in range(4):
                            src = w_main[bass.ds(MAIN0[name] + i * 4 + r, 1), :, :].rearrange("o p n -> (o p) n")
                            load(u0 + i * 4 + r, r, src, DM)
                    if j == 0 and name == "B":
                        body(0)
                        body(1)
                    else:
                        each(sp, 0, count // 4, body)

    @blk.gpsimd
    def _(pool):
        def lo(u, r, n, first=False):
            pool.wait_ge(w_hi_done, u + 1)
            s = r % RING
            pool.tensor_tensor(w_lo[s][:, 0:n], w_raw[s][:, 0:n], f(w_hi[s])[:, 0:n],
                               ALU.subtract).then_inc(w_lo_done, 1)

        def tick(u, r, like):
            if not isinstance(u, int) or u + AHEAD < NU:
                lo(u + AHEAD, r + AHEAD, unit_tiles(like + AHEAD) * P)

        powers = [0]

        def power(rows=P, n=1):
            powers[0] += 1
            pool.wait_ge(msq_ready, powers[0])
            pool.tensor_tensor(rstd[0:rows, 0:n], msq[0:rows, 0:n], nhalf[0:rows, 0:n],
                               ALU.pow).then_inc(rstd_ready, 1)

        pool.memset(nhalf[:, :], -0.5)
        pool.memset(halo_g[:, :, :], 0.0)
        pool.memset(halo_c[:, :, :], 0.0)
        pool.memset(halo_d[:, :, :], 0.0)
        pool.drain().then_inc(halo_zeroed, 1)
        pool.wait_ge(halo_zeroed, 1)
        for u in range(AHEAD):
            lo(u, u, unit_tiles(u) * P)
            power()
        power()
        for j in range(NBLK):
            last = j == NBLK - 1
            for name, count in SECTIONS:
                u0 = j * UPB + UNIT0[name]

                def body(i, like=0):
                    for r in range(4):
                        tick(u0 + i * 4 + r, r, u0 + like * 4 + r)
                n = count // 4
                if name in ("B", "O"):
                    for i in range(n):
                        for r in range(4):
                            u = u0 + i * 4 + r
                            tick(u, u, u)
                            if name == "B" and j and r % 2:
                                power()
                            t = {0: 2, 2: 3, 4: 4}.get(u - u0)
                            if name == "O" and not last and t is not None and t < n_tok(j + 1):
                                power(rows_of(t))
                elif n == 1:
                    body(0)
                else:
                    each(pool, 0, n - 1, body)
                    body(n - 1, n - 1)
                if name == "V":
                    power(n=TPB)
                    if last:
                        power(DEC)
                if name == "G2" and not last:
                    power()
                    power()
        for t in range(n_tok(NBLK - 1)):
            power(rows_of(t))

    @blk.scalar
    def _(act):
        def hi(u, r, n, first=False):
            s = r % RING
            act.wait_ge(w_landed[s], (u // RING + 1) * 16 if isinstance(u, int) else u)
            act.activation(w_hi[s][:, 0:n], w_raw[s][:, 0:n], ACT.Copy).then_inc(w_hi_done, 1)

        def tick(u, r, like):
            if isinstance(u, int) and u + AHEAD >= NU:
                return
            s = (r + AHEAD) % RING
            n = unit_tiles(like + AHEAD) * P
            if not isinstance(u, int) or u >= 1:
                act.wait_ge(acc_done, u)
            act.wait_ge(w_landed[s], (u - r) * (16 // RING) + ((r + AHEAD) // RING + 1) * 16)
            act.activation(w_hi[s][:, 0:n], w_raw[s][:, 0:n], ACT.Copy).then_inc(w_hi_done, 1)

        def done(u):
            act.wait_ge(acc_done, u + 1)

        def sigmoid(j, u, r, q, par, ready, bias=0.0):
            done(u)
            if not isinstance(q, int) or q >= 2:
                act.wait_ge(sig_used, q - 1)
            act.activation(tv(sig[par], j), accv(r % 2, j), ACT.Sigmoid, bias=bias).then_inc(ready, 1)

        def load_x(j, t):
            n = rows_of(t)
            act.dma_start(xt[t % 2][0:n, :], x_rows(j, t)).then_inc(x_loaded[t % 2], 16)

        def load_xres(j, t):
            n = rows_of(t)
            act.dma_start(xres[t % 2][0:n, :], x_rows(j, t)).then_inc(xres_loaded[t % 2], 16)

        stored = [0, 0]

        def store_y(j, t):
            n = rows_of(t)
            act.wait_ge(y_ready, xn(j, t) + 1)
            act.dma_start(y_rows(j, t), xres[t % 2][0:n, :]).then_inc(y_stored[t % 2], 16)
            stored[t % 2] += 1

        def next_xres(j, t):
            if t < n_tok(j):
                act.wait_ge(y_stored[t % 2], 16 * stored[t % 2])
                load_xres(j, t)

        load_x(0, 0)
        load_x(0, 1)
        for dst, src in [(ident[:, :], ident_in), (col[:, :], cols)]:
            act.dma_start(dst, src).then_inc(const_loaded, 16)
        for u in range(AHEAD):
            hi(u, u, unit_tiles(u) * P)
        for dst, src in [(bs_bc[:, :, :], bs_rows.partition_broadcast(P)),
                         (ws[:, :, :], ws_t), (tmp[:, 0:P], mask_t), (poolw[:, :, :], pool_w),
                         (smp_g[:, :, :], st_conv), (smp_c[:, :, :], st_pool), (smp_d[:, :, :], st_short),
                         (g_post_bc[:, :], rows[0:DM].partition_broadcast(P)),
                         (lnv_g_bc[:, :], rows[DM:DM + WB].partition_broadcast(P)),
                         (lnv_b_bc[:, :], rows[DM + WB:DM + 2 * WB].partition_broadcast(P))]:
            act.dma_start(dst, src).then_inc(const_loaded, 16)
        for t in range(2, TPB):
            act.wait_ge(side_done, SIDE["H", 0] + t - 1)
            load_x(0, t)
        act.wait_ge(const_ready, 1)

        for j in range(NBLK):
            last = j == NBLK - 1
            ub = j * UPB
            q0 = j * 56
            u0 = ub + UNIT0["B"]
            for r in range(8):
                u = u0 + r
                tick(u, r, u)
                if r % 2 == 0:
                    sigmoid(j, u, r, q0 + r // 2, (r // 2) % 2, acc_free[r % 2])
                if j and r in (3, 5, 7):
                    t = (r - 3) // 2
                    if t:
                        next_xres(j - 1, t + 1)
                    store_y(j - 1, t)
            u0 = ub + UNIT0["V"]
            for r in range(4):
                tick(u0 + r, r, u0 + r)
                if j and r == 1:
                    store_y(j - 1, TPB - 1)
                done(u0 + r)
                act.activation(tv(vT[:, r, :], j), accv(r % 2, j), ACT.Copy).then_inc(acc_free[r % 2], 1)
            u0 = ub + UNIT0["C"]
            for r in range(8):
                u = u0 + r
                tick(u, r, u)
                c = r // 4 * 2 + r % 2
                if r % 4 < 2:
                    done(u)
                    if j * CT + c >= 2:
                        act.wait_ge(ext_used, j * CT + c - 1)
                    pcs = pieces(j, PH)
                    for n, (t0, m, c0, b, a0) in enumerate(pcs):
                        ins = act.activation(ext[c % 2][:, c0:c0 + m], acc[:, r % 2, b, a0:a0 + m], ACT.Copy)
                    ins.then_inc(acc_free[r % 2], 1)
                else:
                    sigmoid(j, u, r, q0 + 4 + c, c % 2, z_sig_ready)
            u0 = ub + UNIT0["M"]
            for r in range(8):
                u = u0 + r
                c = r // 2
                tick(u, r, u)
                if r % 2 == 0:
                    done(u)
                    if j * 8 + c >= 2:
                        act.wait_ge(cpy_used, j * 8 + c - 1)
                    act.activation(tv(cpy[c % 2], j), accv(0, j), ACT.Copy).then_inc(acc_free[0], 1)
                else:
                    sigmoid(j, u, r, q0 + 8 + c, c % 2, z_sig_ready)
                if last and r == 1:
                    act.wait_ge(vn_ready, j + 1)
                    act.dma_start(v_s, v_n[0:DEC, TPB, :]).then_inc(v_stored, 16)

            def gates(ph, qg):
                u0 = ub + UNIT0[f"G{ph}"]

                def body(i, like=0):
                    for r in range(4):
                        tick(u0 + i * 4 + r, r, u0 + like * 4 + r)
                        if r % 2 == 0:
                            m = i * 2 + r // 2
                            sigmoid(j, u0 + i * 4 + r, r, q0 + qg + m, (r // 2) % 2, acc_free[0],
                                    c1("b_gate", BRANCHES[ph] * KT + m))
                each(act, 0, 3, body)
                body(3, 3)

            gates(0, 12)
            u0 = ub + UNIT0["D"]

            def body_d(i, par, like):
                for r in range(4):
                    u = u0 + i * 4 + r
                    tick(u, r, u0 + like * 4 + r)
                    if r == 0:
                        done(u)
                        act.wait_ge(cpy_used, i + (j * 8 + 4 - 1))
                        act.activation(tv(cpy[par], j), accv(0, j), ACT.Copy).then_inc(acc_free[0], 1)
                    if r == 3:
                        sigmoid(j, u, r, q0 + 20 + i, par, z_sig_ready)
            for i in range(4):
                body_d(i, i % 2, i)
            gates(1, 24)
            u0 = ub + UNIT0["Z"]
            tick(u0, 0, u0)
            act.wait_ge(var_ready, j + 1)
            act.activation(tmp[:, 0:width(j)], tmp[:, 0:width(j)], ACT.Sqrt).then_inc(std_ready, 1)
            for r in range(4):
                if r:
                    tick(u0 + r, r, u0 + r)
                act.wait_ge(ln_ready, j * CT + r + 1)
                act.wait_ge(sig_used, q0 + 32 + 2 * r - 1)
                act.activation(sig[0][:, 0:width(j)], cb[:, r, 0:width(j)], ACT.Sigmoid,
                               bias=c1("ln_b", r), scale=c1("ln_g", r)).then_inc(lnsig_ready, 1)
                sigmoid(j, u0 + r, r, q0 + 32 + 2 * r + 1, 1, z_sig_ready)
            gates(2, 40)
            if not last:
                load_x(j + 1, 0)
                load_x(j + 1, 1)
            gates(3, 48)
            u0 = ub + UNIT0["O"]
            for r in range(8):
                u = u0 + r
                tick(u, r, u)
                done(u)
                act.activation(tv(yT[:, r, :], j), accv(r % 2, j), ACT.Copy).then_inc(acc_free[r % 2], 1)
                if r == 0:
                    if last:
                        act.wait_ge(v_stored, 16)
                    load_xres(j, 0)
                    load_xres(j, 1)
                t = {0: 2, 2: 3, 4: 4}.get(r)
                if not last and t is not None and t < n_tok(j + 1):
                    act.wait_ge(side_done, SIDE["H", j + 1] + t - 1)
                    load_x(j + 1, t)
        for t in range(n_tok(NBLK - 1)):
            if t:
                next_xres(NBLK - 1, t + 1)
            store_y(NBLK - 1, t)
        act.wait_ge(states_ready, 1)
        for dst, src in [(conv_p, halo_g), (pool_p, halo_c), (short_p, halo_d),
                         (conv_s, smp_g), (pool_s, smp_c), (short_s, smp_d)]:
            act.dma_start(dst, src[:, :, :]).then_inc(states_stored, 16)
        act.wait_ge(states_stored, 16 * 6)
        for b in range(2):
            act.wait_ge(y_stored[b], 16 * stored[b])

    @blk.vector
    def _(dve):
        msqs = [0]

        def rms_rstd(view, rows):
            for b in range(2):
                dve.bn_stats(stats[0:rows, b, :], view[0:rows, b * 512:(b + 1) * 512])
            dve.drain()
            dve.bn_aggr(mv[0:rows, 0, :], stats[0:rows, 0:2, :])
            dve.drain()
            dve.scalar_tensor_tensor(msq[0:rows, 1:2], mv[0:rows, 0, 0:1], mv[0:rows, 0, 0:1],
                                     mv[0:rows, 0, 1:2], ALU.mult, ALU.add)
            dve.drain()
            dve.tensor_scalar(msq[0:rows, 0:1], msq[0:rows, 1:2], EPS, None, ALU.add).then_inc(msq_ready, 1)
            msqs[0] += 1
            dve.wait_ge(rstd_ready, msqs[0])

        def x_prep(j, t):
            n, rows = xn(j, t), rows_of(t)
            dve.wait_ge(x_loaded[t % 2], 16 * (xcount(j, t)))
            rms_rstd(xt[t % 2], rows)
            dve.tensor_scalar(xt[t % 2][0:rows, :], xt[t % 2][0:rows, :], rstd[0:rows, 0:1], None,
                              ALU.mult).then_inc(xs_ready, 1)

        def xcount(j, t):
            return j * (TPB // 2) + t // 2 + 1

        def h_out(j, t):
            k, n = SIDE["H", j] + t, rows_of(t)
            dve.wait_ge(side_done, k + 1)
            for b in range(2):
                ps = side[:, k % 2, b * 512:(b + 1) * 512].rearrange("p (a n) -> p a n", n=P)[:, :, 0:n]
                tm = tmp[:, 0:512].rearrange("p (a n) -> p a n", n=P)[:, :, 0:n]
                g = col[:, COLS["g_pre"] + 4 * b:COLS["g_pre"] + 4 * b + 4].unsqueeze(2).to_broadcast([P, 4, n])
                dve.drain()
                dve.tensor_tensor(tm, ps, g, ALU.mult)
                if b:
                    dve.drain().then_inc(side_free, 1)
                else:
                    dve.drain()
                hi = h_hi[:, 4 * b:4 * b + 4, t * P:t * P + n]
                dve.tensor_copy(hi, tm)
                dve.drain()
                ins = dve.tensor_tensor(h_lo[:, 4 * b:4 * b + 4, t * P:t * P + n], tm, f(hi), ALU.subtract)
            ins.then_inc(h_ready, 1)

        def y_out(j, t):
            n = rows_of(t)
            k = SIDE["Y", j + 1] + t
            dve.wait_ge(side_done, k + 1)
            rms_rstd(side[:, k % 2, :], n)
            dve.scalar_tensor_tensor(ynorm[0:n, :], side[0:n, k % 2, :], rstd[0:n, 0:1], g_post_bc[0:n, :],
                                     ALU.mult, ALU.mult)
            dve.drain().then_inc(side_free, 1)
            dve.wait_ge(xres_loaded[t % 2], 16 * xcount(j, t))
            dve.tensor_tensor(xres[t % 2][0:n, :], xres[t % 2][0:n, :], ynorm[0:n, :],
                              ALU.add).then_inc(y_ready, 1)

        def ready_at(s, half):
            dve.wait_ge(acc_free[s], half + 1)

        def result(j, buf, c, semaphore=None, before=None):
            w = width(j)
            hi = out_hi[buf][:, bass.ds(c, 1), 0:w].rearrange("p o w -> p (o w)")
            lo = out_lo[buf][:, bass.ds(c, 1), 0:w].rearrange("p o w -> p (o w)")
            dve.tensor_copy(hi, tmp[:, 0:w])
            if before is not None:
                dve.drain().then_inc(before, 1)
            else:
                dve.drain()
            dve.tensor_tensor(lo, tmp[:, 0:w], f(hi), ALU.subtract).then_inc(res_ready, 1)

        def conv_step(j, t):
            dve.drain()
            for c in range(CT):
                for t0, n, c0 in segments(j, CH):
                    src = glu[:, c, bass.ds(c0 - CH + t, n)]
                    dst = cb[:, c, t0:t0 + n]
                    if isinstance(t, int) and t == 0:
                        dve.tensor_scalar(dst, src, c1("conv_w", c * CK), c1("conv_bias", c), ALU.mult, ALU.add)
                    else:
                        dve.scalar_tensor_tensor(dst, src, c1("conv_w", c * CK + t), dst, ALU.mult, ALU.add)

        dve.memset(mean_mat[:, :], 1.0 / WB)
        dve.wait_ge(const_loaded, 16 * 12)
        dve.tensor_tensor(ws[:, :, :], ws[:, :, :], tmp[:, 0:P].unsqueeze(1).to_broadcast([P, CT, P]), ALU.mult)
        dve.wait_ge(halo_zeroed, 1)
        dve.drain().then_inc(const_ready, 1)
        for t in range(TPB):
            x_prep(0, t)
            h_out(0, t)

        for j in range(NBLK):
            last = j == NBLK - 1
            ub = j * UPB
            w = width(j)
            segs = segments(j, CH)
            dve.tensor_copy(glu[:, :, 0:CH], halo_g[:, :, :])
            if last:
                dve.tensor_copy(glu[:, :, CH + BLK:2 * CH + BLK], smp_g[:, :, :])
            for c in range(CT):
                u = ub + UNIT0["B"] + 2 * c
                ready_at(0, u // 2)
                dve.wait_ge(acc_done, u + 2)
                for t0, m, c0, b, a0 in pieces(j, CH):
                    ins = dve.tensor_tensor(glu[:, c, c0:c0 + m], acc[:, 1, b, a0:a0 + m],
                                            sig[c % 2][:, t0:t0 + m], ALU.mult)
                ins.then_inc(acc_free[1], 1)
                dve.drain().then_inc(sig_used, 1)
                if j:
                    y_out(j - 1, c)
            dve.drain()
            dve.tensor_copy(halo_g[:, :, :], glu[:, :, BLK:BLK + CH])
            if last:
                dve.tensor_copy(smp_g[:, :, :], glu[:, :, CH + BLK + DEC:2 * CH + BLK + DEC])
            for t in range(3):
                conv_step(j, t)
            k = SIDE["V", j]
            dve.wait_ge(side_done, k + 2)

            def v_tile(t):
                if t == TPB:
                    return side[0:DEC, (k + 2) % 2, 0:WB]
                return side[:, (k + t // 2) % 2, t % 2 * 512:t % 2 * 512 + WB]

            for t in range(TPB):
                dve.bn_stats(stats[:, t, :], v_tile(t))
            dve.drain()
            for t in range(TPB):
                dve.bn_aggr(mv[:, t, :], stats[:, t, :])
            dve.drain()
            dve.tensor_scalar(msq[:, 0:TPB], mv[:, 0:TPB, 1], EPS, None, ALU.add).then_inc(msq_ready, 1)
            msqs[0] += 1
            dve.wait_ge(rstd_ready, msqs[0])
            if j:
                for b in range(2):
                    dve.wait_ge(y_stored[b], 16 * (TPB // 2) * j)

            def v_norm(t, n, r):
                dve.tensor_scalar(v_n[0:n, t, :], v_tile(t), mv[0:n, t, 0:1], rstd[0:n, r:r + 1],
                                  ALU.subtract, ALU.mult)

            def v_affine(t, n):
                dve.tensor_tensor(v_n[0:n, t, :], v_n[0:n, t, :], lnv_g_bc[0:n, :], ALU.mult)
                dve.drain()
                dve.tensor_tensor(v_n[0:n, t, :], v_n[0:n, t, :], lnv_b_bc[0:n, :], ALU.add)

            for t in range(TPB):
                v_norm(t, P, t)
                if t % 2:
                    dve.drain().then_inc(side_free, 1)
            for t in range(TPB):
                v_affine(t, P)
            if last:
                dve.wait_ge(side_done, k + 3)
                dve.bn_stats(stats[0:DEC, TPB, :], v_tile(TPB))
                dve.drain()
                dve.bn_aggr(mv[0:DEC, TPB, :], stats[0:DEC, TPB, :])
                dve.drain()
                dve.tensor_scalar(msq[0:DEC, 0:1], mv[0:DEC, TPB, 1:2], EPS, None, ALU.add).then_inc(msq_ready, 1)
                msqs[0] += 1
                dve.wait_ge(rstd_ready, msqs[0])
                v_norm(TPB, DEC, 0)
                dve.drain().then_inc(side_free, 1)
                v_affine(TPB, DEC)
            dve.drain().then_inc(vn_ready, 1)

            def pool_chunk(c):
                e = ext[c % 2]
                length = BLK + PH + (PH + DEC if last else 0)
                ready_at(c % 2, (ub + UNIT0["C"]) // 2 + c // 2 * 2)
                src, bufs = e, [win_a, win_b]
                for s in range(c + 1):
                    d = 1 << s
                    lo = 2 * d - 1
                    dst = bufs[s % 2]
                    dve.tensor_tensor(dst[:, lo:length], src[:, lo:length], src[:, lo - d:length - d], ALU.add)
                    dve.drain()
                    src = dst
                win = 2 << c
                ps = pooled[c % 2]
                for t0, n, c0 in segments(j, PH):
                    dve.scalar_tensor_tensor(ps[:, t0:t0 + n], src[:, c0:c0 + n], 1.0 / win, e[:, c0:c0 + n],
                                             ALU.mult, ALU.subtract)
                if j == 0:
                    dve.drain()
                    m = win - 1
                    iv = COLS["inv_count"]
                    dve.tensor_tensor(ps[:, 0:m], src[:, PH:PH + m], col[:, iv:iv + m], ALU.mult)
                    dve.drain()
                    dve.tensor_tensor(ps[:, 0:m], ps[:, 0:m], e[:, PH:PH + m], ALU.subtract)
                dve.drain().then_inc(pooled_ready, 1)
                dve.tensor_copy(halo_c[:, c, :], e[:, BLK:BLK + PH])
                if last:
                    dve.tensor_copy(smp_c[:, c, :], e[:, PH + BLK + DEC:2 * PH + BLK + DEC])
                dve.drain().then_inc(ext_used, 1)

            for i in range(2):
                for c in (2 * i, 2 * i + 1):
                    dve.tensor_copy(ext[c % 2][:, 0:PH], halo_c[:, c, :])
                    if last:
                        dve.tensor_copy(ext[c % 2][:, PH + BLK:2 * PH + BLK], smp_c[:, c, :])
                    dve.drain()
                    pool_chunk(c)
                for c in (2 * i, 2 * i + 1):
                    u = ub + UNIT0["C"] + 4 * i + 2 + c % 2
                    dve.wait_ge(z_sig_ready, j * 16 + c + 1)
                    dve.tensor_tensor(tv(sig[c % 2], j), accv(u % 2, j), tv(sig[c % 2], j),
                                      ALU.mult).then_inc(acc_free[u % 2], 1)
                    k = SIDE["P", j] + c
                    dve.wait_ge(side_done, k + 1)
                    dve.drain()
                    dve.scalar_tensor_tensor(tmp[:, 0:w], side[:, k % 2, 0:w], c1("pool_scale", c),
                                             sig[c % 2][:, 0:w], ALU.mult, ALU.mult)
                    dve.drain().then_inc(side_free, 1)
                    result(j, 0, c, before=sig_used)
                    conv_step(j, 3 + c)
            for c in range(CT):
                u = ub + UNIT0["M"] + 2 * c
                k = SIDE["M", j] + c
                dve.wait_ge(side_done, k + 1)
                dve.drain()
                dve.tensor_tensor(tmp[:, 0:BLK].rearrange("p (a t) -> p a t", t=P),
                                  side[:, k % 2, 0:BLK].rearrange("p (a t) -> p a t", t=P),
                                  bs_bc[:, c, :].unsqueeze(1).to_broadcast([P, TPB, P]), ALU.add)
                if last:
                    dve.tensor_tensor(tmp[:, BLK:WMAX], side[:, k % 2, BLK:WMAX], bs_bc[:, c, 0:DEC], ALU.add)
                dve.drain().then_inc(side_free, 1)
                ready_at(0, u // 2)
                dve.tensor_tensor(tmp[:, 0:w], tmp[:, 0:w], cpy[c % 2][:, 0:w], ALU.mult)
                dve.drain().then_inc(cpy_used, 1)
                dve.wait_ge(z_sig_ready, j * 16 + 4 + c + 1)
                dve.tensor_tensor(tv(sig[c % 2], j), accv(1, j), tv(sig[c % 2], j),
                                  ALU.mult).then_inc(acc_free[1], 1)
                dve.drain()
                dve.tensor_tensor(tmp[:, 0:w], tmp[:, 0:w], sig[c % 2][:, 0:w], ALU.mult)
                dve.drain().then_inc(sig_used, 1)
                result(j, 1, c)
                conv_step(j, 7 + c)

            def merge(ph, start, end, with_conv=False, split=False):
                u0 = ub + UNIT0[f"G{ph}"]

                def body(i):
                    for r in range(2):
                        m = i * 2 + r
                        half = i * 2 + (u0 // 2 + r)
                        ready_at(0, half)
                        dve.wait_ge(acc_done, i * 4 + (u0 + 2 * r + 2))
                        dst = merged[:, bass.ds(m, 1), 0:w].rearrange("p o w -> p (o w)")
                        if ph == 0:
                            dve.tensor_tensor(tv(dst, j), accv(1, j), tv(sig[r], j),
                                              ALU.mult).then_inc(acc_free[1], 1)
                            dve.drain().then_inc(sig_used, 1)
                        else:
                            dve.tensor_tensor(tv(tmp, j), accv(1, j), tv(sig[r], j),
                                              ALU.mult).then_inc(acc_free[1], 1)
                            dve.drain().then_inc(sig_used, 1)
                            dve.tensor_tensor(dst, dst, tmp[:, 0:w], ALU.add)
                            if split:
                                dve.drain()
                                split_merged(m)
                        if with_conv:
                            conv_step(j, m + 11)
                        dve.drain()
                dve.drain()
                each(dve, start, end, body)

            def split_merged(m):
                if isinstance(m, int):
                    b, c = m // CT, m % CT
                else:
                    b, c = 0, m
                src = merged[:, bass.ds(m, 1), 0:w].rearrange("p o w -> p (o w)")
                hi = out_hi[b][:, bass.ds(c, 1), 0:w].rearrange("p o w -> p (o w)")
                lo = out_lo[b][:, bass.ds(c, 1), 0:w].rearrange("p o w -> p (o w)")
                dve.tensor_copy(hi, src)
                dve.drain()
                dve.tensor_tensor(lo, src, f(hi), ALU.subtract).then_inc(merge_ready, 1)

            merge(0, 0, 4, with_conv=True)

            def body_d(i, par):
                u = ub + UNIT0["D"]
                e = ext[0]
                dve.tensor_copy(e[:, 0:SH], halo_d[:, i, :])
                if last:
                    dve.tensor_copy(e[:, SH + BLK:2 * SH + BLK], smp_d[:, i, :])
                half = u // 2 + 2 * i
                ready_at(0, half)
                dve.wait_ge(acc_done, u + 4 * i + 2)
                for t0, m, c0, b, a0 in pieces(j, SH):
                    ins = dve.tensor_tensor(e[:, c0:c0 + m], acc[:, 1, b, a0:a0 + m], cpy[par][:, t0:t0 + m],
                                            ALU.mult)
                ins.then_inc(acc_free[1], 1)
                dve.drain().then_inc(cpy_used, 1)
                for tap in range(3):
                    for t0, m, c0 in segments(j, SH):
                        src, dst = e[:, c0 - SH + tap:c0 - SH + tap + m], tmp[:, t0:t0 + m]
                        if tap == 0:
                            dve.tensor_scalar(dst, src, c1("short_w", i * 3), None, ALU.mult)
                        else:
                            dve.scalar_tensor_tensor(dst, src, c1("short_w", i * 3 + tap), dst, ALU.mult, ALU.add)
                    dve.drain()
                dve.tensor_copy(halo_d[:, i, :], e[:, BLK:BLK + SH])
                if last:
                    dve.tensor_copy(smp_d[:, i, :], e[:, SH + BLK + DEC:2 * SH + BLK + DEC])
                conv_step(j, 19 + 3 * i)
                dve.wait_ge(acc_done, u + 4 * i + 3)
                dve.tensor_tensor(tv(tmp, j), accv(0, j), tv(tmp, j), ALU.mult).then_inc(acc_free[0], 1)
                conv_step(j, 20 + 3 * i)
                dve.wait_ge(z_sig_ready, j * 16 + 8 + i + 1)
                dve.tensor_tensor(tv(sig[par], j), accv(1, j), tv(sig[par], j),
                                  ALU.mult).then_inc(acc_free[1], 1)
                dve.drain()
                dve.tensor_tensor(tmp[:, 0:w], tmp[:, 0:w], sig[par][:, 0:w], ALU.mult)
                dve.drain().then_inc(sig_used, 1)
                result(j, 0, i)
                conv_step(j, 21 + 3 * i)
            for i in range(CT):
                body_d(i, i % 2)

            dve.drain()
            dve.tensor_tensor(win_b[:, 0:w], cb[:, 0, 0:w], cb[:, 1, 0:w], ALU.add)
            for c in (2, 3):
                dve.drain()
                ins = dve.tensor_tensor(win_b[:, 0:w], win_b[:, 0:w], cb[:, c, 0:w], ALU.add)
            ins.then_inc(sums_ready, 1)
            merge(1, 0, 2)
            k = SIDE["L", j]
            dve.wait_ge(side_done, k + 1)
            for c in range(CT):
                dve.tensor_tensor(cb[:, c, 0:w], cb[:, c, 0:w], side[:, k % 2, 0:w], ALU.subtract)
            dve.drain().then_inc(side_free, 1)
            dve.tensor_tensor(win_b[:, 0:w], cb[:, 0, 0:w], cb[:, 0, 0:w], ALU.mult)
            for c in (1, 2, 3):
                dve.tensor_tensor(tmp[:, 0:w], cb[:, c, 0:w], cb[:, c, 0:w], ALU.mult)
                dve.drain()
                ins = dve.tensor_tensor(win_b[:, 0:w], win_b[:, 0:w], tmp[:, 0:w], ALU.add)
                if c < 3:
                    dve.drain()
            ins.then_inc(sums_ready, 1)
            merge(1, 2, 4)
            dve.wait_ge(side_done, k + 2)
            dve.tensor_scalar(tmp[:, 0:w], side[:, (k + 1) % 2, 0:w], EPS, None, ALU.add).then_inc(var_ready, 1)
            dve.drain().then_inc(side_free, 1)
            dve.wait_ge(std_ready, j + 1)
            dve.reciprocal(win_b[:, 0:w], tmp[:, 0:w])
            dve.drain()
            for c in range(CT):
                dve.tensor_tensor(cb[:, c, 0:w], cb[:, c, 0:w], win_b[:, 0:w], ALU.mult).then_inc(ln_ready, 1)
            for c in range(CT):
                u = ub + UNIT0["Z"] + c
                dve.wait_ge(lnsig_ready, j * CT + c + 1)
                dve.tensor_scalar(cb[:, c, 0:w], cb[:, c, 0:w], c1("ln_g", c), c1("ln_b", c), ALU.mult, ALU.add)
                dve.drain()
                dve.tensor_tensor(tmp[:, 0:w], cb[:, c, 0:w], sig[0][:, 0:w], ALU.mult)
                dve.drain().then_inc(sig_used, 1)
                dve.wait_ge(z_sig_ready, j * 16 + 12 + c + 1)
                dve.tensor_tensor(tv(sig[1], j), accv(u % 2, j), tv(sig[1], j), ALU.mult).then_inc(acc_free[u % 2], 1)
                dve.drain()
                dve.tensor_tensor(tmp[:, 0:w], tmp[:, 0:w], sig[1][:, 0:w], ALU.mult)
                dve.drain().then_inc(sig_used, 1)
                result(j, 1, c)
            dve.drain()
            merge(2, 0, 4)
            if not last:
                x_prep(j + 1, 0)
                x_prep(j + 1, 1)
            merge(3, 0, 2, split=True)
            merge(3, 2, 4)
            for m in range(CT, KT):
                split_merged(m)
            dve.drain()
            if not last:
                for t in range(n_tok(j + 1)):
                    h_out(j + 1, t)
                    if t + 2 < n_tok(j + 1):
                        x_prep(j + 1, t + 2)
        dve.drain().then_inc(states_ready, 1)
        for t in range(n_tok(NBLK - 1)):
            y_out(NBLK - 1, t)

    @blk.tensor
    def _(pe):
        def run_unit(j, u, half, r, rhs_hi, rhs_lo, nk, per_k=None):
            s, slot = r % 2, r % RING
            if not isinstance(half, int) or half >= 1:
                pe.wait_ge(acc_free[s], half)
            pe.wait_ge(w_lo_done, u + 1)
            for k in range(nk):
                if per_k:
                    per_k(k)
                wk = slice(k * P, (k + 1) * P)
                for n, (wt, mv_) in enumerate([(w_hi, rhs_hi), (w_hi, rhs_lo), (w_lo, rhs_hi)]):
                    for b, (t0, m) in enumerate(tiles(j)):
                        ins = pe.matmul(acc[:, s, b, 0:m], wt[slot][:, wk], mv_[:, k, t0:t0 + m],
                                        start=(k == 0 and n == 0), stop=(k == nk - 1 and n == 2))
            ins.then_inc(acc_done, 1)

        def section(j, name, start, end, body):
            u0 = j * UPB + UNIT0[name]
            if j == 0 and name == "B":
                for i in range(start, end):
                    body(i, u0 + 4 * i, u0 // 2 + 2 * i)
            else:
                each(pe, start, end, lambda i: body(i, i * 4 + u0, i * 2 + u0 // 2))

        def full(j):
            return lambda i, u, half, r: run_unit(j, u + r, half + r // 2, r, h_hi, h_lo, KT)

        def slot_free(k):
            if not isinstance(k, int) or k >= 2:
                pe.wait_ge(side_free, k - 1)

        def h_job(j, t):
            k, n = SIDE["H", j] + t, rows_of(t)
            slot_free(k)
            pe.wait_ge(xs_ready, xn(j, t) + 1)
            for c in range(KT):
                ins = pe.transpose(side[:, k % 2, c * P:c * P + n], xt[t % 2][0:n, c * P:(c + 1) * P],
                                   ident[0:n, 0:n])
            ins.then_inc(side_done, 1)

        def y_job(j, t, k, par):
            n = rows_of(t) if isinstance(t, int) else P
            slot_free(k)
            for c in range(KT):
                src = yT[:, c, bass.ds(t * P, n)] if isinstance(t, int) else None
                ins = pe.transpose(side[0:n, par, c * P:(c + 1) * P], src, ident[:, :])
            ins.then_inc(side_done, 1)

        pe.wait_ge(const_loaded, 16 * 12)
        for t in range(TPB):
            h_job(0, t)
        pe.wait_ge(const_ready, 1)
        hcount = 0
        for j in range(NBLK):
            last = j == NBLK - 1
            w = width(j)
            hcount += n_tok(j)
            pe.wait_ge(h_ready, hcount)
            fu = full(j)
            ub = j * UPB
            for i in range(2):
                for r in range(4):
                    u = ub + 4 * i + r
                    run_unit(j, u, u // 2, r, h_hi, h_lo, KT)
                    if r % 2 and j:
                        t = 2 * i + r // 2
                        k = SIDE["Y", j] + t
                        if t == 0:
                            pe.wait_ge(acc_free[0], ub // 2)
                            pe.wait_ge(acc_free[1], ub // 2)
                        y_job(j - 1, t, k, k % 2)
            u = ub + UNIT0["V"]
            for r in range(4):
                run_unit(j, u + r, (u + r) // 2, r, h_hi, h_lo, KT)
            k = SIDE["V", j]
            slot_free(k + 1)
            for c in range(CT):
                pe.wait_ge(acc_free[c % 2], (u + c) // 2 + 1)
                for t in range(TPB):
                    s = (k + t // 2) % 2
                    ins = pe.transpose(side[:, s, t % 2 * 512 + c * P:t % 2 * 512 + (c + 1) * P],
                                       vT[:, c, t * P:(t + 1) * P], ident[:, :])
                    if c == CT - 1 and t % 2:
                        ins.then_inc(side_done, 1)
            if last:
                slot_free(k + 2)
                for c in range(CT):
                    ins = pe.transpose(side[0:DEC, (k + 2) % 2, c * P:(c + 1) * P], vT[:, c, BLK:WMAX], ident[:, :])
                ins.then_inc(side_done, 1)

            for i in range(2):
                for r in range(4):
                    u = ub + UNIT0["C"] + 4 * i + r
                    run_unit(j, u, u // 2, r, h_hi, h_lo, KT)
                    if r >= 2:
                        c = 2 * i + r - 2
                        k = SIDE["P", j] + c
                        slot_free(k)
                        pe.wait_ge(pooled_ready, j * CT + c + 1)
                        for t0, m in side_pieces(j):
                            ins = pe.matmul(side[:, k % 2, t0:t0 + m], poolw[:, c, :], pooled[c % 2][:, t0:t0 + m],
                                            start=True, stop=True)
                        ins.then_inc(side_done, 1)
            for c in range(CT):
                u = ub + UNIT0["M"] + 2 * c
                run_unit(j, u, u // 2, u % RING, h_hi, h_lo, KT)
                k = SIDE["M", j] + c
                slot_free(k)
                pe.wait_ge(vn_ready, j + 1)
                for t in range(n_tok(j)):
                    n = rows_of(t)
                    ins = pe.matmul(side[:, k % 2, t * P:t * P + n], v_n[0:n, t, c * P:(c + 1) * P],
                                    ws[0:n, c, 0:n], start=True, stop=True)
                ins.then_inc(side_done, 1)
                run_unit(j, u + 1, u // 2, (u + 1) % RING, h_hi, h_lo, KT)

            def gated(ph, start, end):
                b = OUTBUF[ph]

                def body(i, u, half):
                    for r in (0, 2):
                        run_unit(j, u + r, half + r // 2, r, h_hi, h_lo, KT)
                        run_unit(j, u + r + 1, half + r // 2, r + 1, out_hi[b], out_lo[b], CT)
                if start == 0:
                    pe.wait_ge(res_ready, 16 * j + 4 * ph + 4)
                section(j, f"G{ph}", start, end, body)

            def l_job(k, n):
                slot_free(k)
                pe.wait_ge(sums_ready, n)
                for t0, m in side_pieces(j):
                    ins = pe.matmul(side[:, k % 2, t0:t0 + m], mean_mat[:, :], win_b[:, t0:t0 + m],
                                    start=True, stop=True)
                ins.then_inc(side_done, 1)

            def body4(i, u, half):
                for r in range(4):
                    run_unit(j, u + r, half + r // 2, r, h_hi, h_lo, KT)

            gated(0, 0, 4)
            section(j, "D", 0, 4, body4)
            gated(1, 0, 2)
            l_job(SIDE["L", j], 2 * j + 1)
            gated(1, 2, 4)
            l_job(SIDE["L", j] + 1, 2 * j + 2)
            section(j, "Z", 0, 1, body4)
            gated(2, 0, 4)
            gated(3, 0, 4)
            if not last:
                h_job(j + 1, 0)
                h_job(j + 1, 1)

            def rhs_k(parts, k):
                return parts[k // CT][:, k % CT, :]

            for m in range(KT):
                u = ub + UNIT0["O"] + m
                s, slot = m % 2, m % RING
                pe.wait_ge(acc_free[s], u // 2)
                pe.wait_ge(w_lo_done, u + 1)
                for k in range(KT):
                    if m == 0:
                        pe.wait_ge(merge_ready, j * KT + k + 1)
                    for n, (wt, parts) in enumerate([(w_hi, out_hi), (w_hi, out_lo), (w_lo, out_hi)]):
                        for b, (t0, mm) in enumerate(tiles(j)):
                            ins = pe.matmul(acc[:, s, b, 0:mm], wt[slot][:, k * P:(k + 1) * P],
                                            rhs_k(parts, k)[:, t0:t0 + mm],
                                            start=(k == 0 and n == 0), stop=(k == KT - 1 and n == 2))
                ins.then_inc(acc_done, 1)
                if not last and m in (1, 3, 5) and m // 2 + 2 < n_tok(j + 1):
                    h_job(j + 1, m // 2 + 2)
        pe.wait_ge(acc_free[0], NU // 2)
        pe.wait_ge(acc_free[1], NU // 2)
        for t in range(n_tok(NBLK - 1)):
            k = SIDE["Y", NBLK] + t
            y_job(NBLK - 1, t, k, k % 2)

    block.__exit__(None, None, None)


_OUTS = [("y_prompt", (SEQ, DM)), ("y_sample", (DEC, DM)), ("conv_p", (P, CT, CH)), ("pool_p", (P, CT, PH)),
         ("short_p", (P, CT, SH)), ("conv_s", (P, CT, CH)), ("pool_s", (P, CT, PH)), ("short_s", (P, CT, SH)),
         ("v_s", (DEC, WB))]


def kernel(x_prompt, x_sample, state_conformer_conv, state_pool, state_short_conv, g_pre, g_post, w_in,
           b_gate, ln_v_g, ln_v_b, w_s, b_s, conv_b_w, conv_b_bias, ln_b_g, ln_b_b, pool_w, pool_scale,
           conv_d_w, w_branch, w_out):
    import numpy as np
    import concourse.bacc as bacc
    from concourse.bass_utils import run_bass_kernel_spmd

    def tiles_of(w, c0):
        k = w.shape[0] // P
        return w[:, c0:c0 + P].reshape(k, P, P).transpose(1, 0, 2).reshape(P, k * P)

    w_in, w_br, w_o = (np.asarray(a)[0] for a in (w_in, w_branch, w_out))
    part = lambda p, c: tiles_of(w_in, p * WB + c * P)
    gate = lambda b, m: tiles_of(w_in, 12 * WB + b * DM + m * P)
    main = []
    for name, _ in SECTIONS:
        if name == "B":
            main += [part(p, c) for c in range(CT) for p in (B_B, B_A)]
        elif name == "V":
            main += [part(A_V, c) for c in range(CT)]
        elif name == "C":
            main += [part(p, 2 * i + c) for i in range(2) for p in (C_X, C_Z) for c in range(2)]
        elif name == "M":
            main += [part(p, c) for c in range(CT) for p in (A_U, A_Z)]
        elif name == "D":
            main += [part(p, c) for c in range(CT) for p in (D_C, D_X, D_B, D_Z)]
        elif name == "Z":
            main += [part(B_Z, c) for c in range(CT)]
        elif name == "O":
            main += [tiles_of(w_o, m * P) for m in range(KT)]
        else:
            main += [gate(BRANCHES[int(name[1])], m) for m in range(KT)]
    chan = lambda a: np.asarray(a).reshape(-1, P).T
    taps = lambda a: np.asarray(a)[0].reshape(-1, CT, P).transpose(2, 1, 0)
    inv_count = np.broadcast_to(1.0 / np.arange(1, 17, dtype=np.float32), (P, 16))
    cols = np.concatenate([chan(b_gate), taps(conv_b_w).reshape(P, -1), chan(conv_b_bias), chan(ln_b_g),
                           chan(ln_b_b), chan(pool_scale), taps(conv_d_w).reshape(P, -1), chan(g_pre),
                           inv_count], axis=1)
    arrays = {
        "x_prompt": np.asarray(x_prompt)[0], "x_sample": np.asarray(x_sample)[0],
        "w_main": np.stack(main),
        "w_branch": np.stack([tiles_of(w_br[b], m * P) for b in BRANCHES for m in range(KT)]),
        "cols": cols,
        "rows": np.concatenate([np.asarray(a).reshape(-1) for a in (g_post, ln_v_g, ln_v_b)]),
        "bs_rows": np.asarray(b_s)[0],
        "ws_t": np.asarray(w_s)[0].transpose(2, 0, 1),
        "mask_t": np.triu(np.ones((P, P), np.float32)),
        "pool_w": np.asarray(pool_w)[0].transpose(1, 0, 2),
        "ident": np.eye(P, dtype=np.float32),
        "st_conv": taps(state_conformer_conv[0]), "st_pool": taps(state_pool[0]),
        "st_short": taps(state_short_conv[0]),
    }
    nc = bacc.Bacc("TRN2", target_bir_lowering=False, num_devices=1)
    ins, args = {}, []
    for name, a in arrays.items():
        a = np.ascontiguousarray(a)
        ins[f"in_{name}"] = a
        args.append(nc.dram_tensor(f"in_{name}", a.shape, mybir.dt.from_np(a.dtype), kind="ExternalInput").ap())
    for name, shape in _OUTS:
        args.append(nc.dram_tensor(f"out_{name}", shape, F32, kind="ExternalOutput").ap())
    build(nc, *args)
    r = run_bass_kernel_spmd(nc, [ins], core_ids=[0]).results[0]
    got = {name: r[f"out_{name}"] for name, _ in _OUTS}
    rows_back = lambda a: a.transpose(2, 1, 0).reshape(1, 1, a.shape[2], WB)
    return (got["y_prompt"].reshape(1, SEQ, DM), got["y_sample"].reshape(1, DEC, DM),
            rows_back(got["conv_p"]), rows_back(got["pool_p"]), rows_back(got["short_p"]),
            rows_back(got["conv_s"]), rows_back(got["pool_s"]), rows_back(got["short_s"]),
            got["v_s"].reshape(1, 1, DEC, WB))
```

```python
import concourse.bass as bass
from concourse import mybir

F32 = mybir.dt.float32
F32R = mybir.dt.float32r
ALU = mybir.AluOpType
ACT = mybir.ActivationFunctionType

P = 128
DM = 1024
WB = 512
SEQ = 2048
DEC = 64
KT = DM // P
CT = WB // P
CK = 31
CH = CK - 1
PH = 15
SH = 2
EPS = 1e-6
BLK = 512
NBLK = SEQ // BLK
WMAX = BLK + DEC
RING = 4
AHEAD = RING - 1

SECTIONS = [("B", 8), ("V", 4), ("C", 8), ("M", 8), ("G0", 16), ("D", 16), ("G1", 16), ("Z", 4),
            ("G2", 16), ("G3", 16), ("O", 8)]
UNIT0, MAIN0 = {}, {}
_u = _m = 0
for _n, _c in SECTIONS:
    UNIT0[_n], MAIN0[_n] = _u, _m
    _u += _c
    _m += _c // 2 if _n[0] == "G" else _c
UPB, MAIN = _u, _m
NU = UPB * NBLK
A_U, A_V, A_Z, B_A, B_B, B_Z, C_X, C_Z, D_B, D_C, D_X, D_Z = range(12)
BRANCHES = [2, 0, 3, 1]
OUTBUF = [0, 1, 0, 1]
COLS = {}
_o = 0
for _n, _c in [("b_gate", 4 * KT), ("conv_w", CT * CK), ("conv_bias", CT), ("ln_g", CT), ("ln_b", CT),
               ("pool_scale", CT), ("short_w", CT * 3), ("g_pre", KT), ("g_post", KT),
                ("inv_count", 16)]:
    COLS[_n] = _o
    _o += _c
NCOLS = _o


def half_unit(u):
    r = u % UPB
    return any(n[0] == "G" and UNIT0[n] <= r < UNIT0[n] + c and (r - UNIT0[n]) % 2 for n, c in SECTIONS)


def unit_tiles(u):
    return CT if half_unit(u) else KT


def side_jobs():
    first, k = {}, 0
    first["H", 0] = k
    k += 2
    for j in range(NBLK):
        last = j == NBLK - 1
        for name, n in [("Y", 2 if j else 0), ("V", 3 if last else 2), ("P", CT), ("M", CT), ("L", 3),
                        ("H", 0 if last else 2)]:
            first[name, j + (name == "H")] = k
            k += n
    first["Y", NBLK] = k
    return first


SIDE = side_jobs()


def build(nc, x_t, w_main, w_branch, cols, rows, bs_rows, ws_t, mask_t, pool_w, ident_in,
          st_conv, st_pool, st_short, y_t, conv_p, pool_p, short_p, conv_s, pool_s,
          short_s, v_s):
    at = [0]

    def sb(name, shape, dt=F32, addr=None):
        n = 4
        for s in shape[1:]:
            n *= s
        if addr is None:
            addr = at[0]
            at[0] += (n + 31) // 32 * 32
        return nc.alloc_sbuf_tensor_at(name, list(shape), dt, offset=addr).ap()

    at[0] = (nc.sbuf_base + 31) // 32 * 32
    h_hi, h_lo = sb("h_hi", [P, KT, WMAX], F32R), sb("h_lo", [P, KT, WMAX], F32R)
    out_hi = [sb(f"out_hi{b}", [P, CT, WMAX], F32R) for b in range(2)]
    out_lo = [sb(f"out_lo{b}", [P, CT, WMAX], F32R) for b in range(2)]
    w_raw = [sb(f"w_raw{s}", [P, DM]) for s in range(RING)]
    w_hi = [sb(f"w_hi{s}", [P, DM], F32R) for s in range(RING)]
    w_lo = [sb(f"w_lo{s}", [P, DM], F32R) for s in range(RING)]
    GL = CH + BLK + CH + DEC
    glu = sb("glu", [P, CT, GL])
    cb = sb("cb", [P, CT, WMAX])
    mg_lo, mg_hi = (sb(n, [P, CT, WMAX], F32R, addr=at[0] - o) for n, o in
                    (("mg_lo", (CT * GL + CT * WMAX) * 4), ("mg_hi", CT * WMAX * 4)))
    merged_hi, merged_lo = [out_hi[0], mg_hi], [out_lo[0], mg_lo]
    EL = PH + BLK + PH + DEC + 2
    a = at[0]
    merged = sb("merged", [P, KT, WMAX])
    yT = sb("yT", [P, KT, WMAX], addr=a)
    vT = sb("vT", [P, CT, WMAX], addr=a)
    a += CT * WMAX * 4
    win_a = sb("win_a", [P, EL], addr=a)
    pooled = [sb(f"pooled{b}", [P, WMAX], addr=a + EL * 4 + b * WMAX * 4) for b in range(2)]
    a = at[0]
    xr = sb("xr", [P, KT, WMAX])
    cpy = [sb(f"cpy{b}", [P, WMAX], addr=a + b * WMAX * 4) for b in range(2)]
    win_b = sb("win_b", [P, EL], addr=a + 2 * WMAX * 4)
    v_n = sb("v_n", [P, BLK // P + 1, WB], addr=a + KT * WMAX * 4 - (BLK // P + 1) * WB * 4)
    sig = [sb(f"sig{b}", [P, WMAX]) for b in range(2)]
    a = at[0]
    ext = [sb(f"ext{b}", [P, EL]) for b in range(2)]
    sq_x = sb("sq_x", [P, WMAX], addr=a)
    sq_y = sb("sq_y", [P, WMAX], addr=a + EL * 4)
    tmp = sb("tmp", [P, WMAX])
    diag = sb("diag", [P, BLK // P + 1, P])
    ones = sb("ones", [P, P])
    mean_dm = sb("mean_dm", [P, 2])
    lnv_g_bc, lnv_b_bc = sb("lnv_g_bc", [P, WB]), sb("lnv_b_bc", [P, WB])
    bs_bc = sb("bs_bc", [P, CT, P])
    ws = sb("ws", [P, CT, P])
    poolw = sb("poolw", [P, CT, P])
    ident = sb("ident", [P, P])
    mean_mat = sb("mean_mat", [P, P])
    col = sb("col", [P, NCOLS])
    halo_g, halo_c, halo_d = (sb(f"halo_{n}", [P, CT, w]) for n, w in (("g", CH), ("c", PH), ("d", SH)))
    smp_g, smp_c, smp_d = (sb(f"smp_{n}", [P, CT, w]) for n, w in (("g", CH), ("c", PH), ("d", SH)))
    stats = sb("stats", [P, 8, 6])
    mv = sb("mv", [P, 8, 2])
    msq = sb("msq", [P, 8])
    rstd = sb("rstd", [P, 8])
    nhalf = sb("nhalf", [P, 8])
    assert at[0] <= nc.sbuf_usable_end, (at[0], nc.sbuf_usable_end)
    acc = nc.alloc_psum_tensor("acc", [P, 2, 2, 512], F32).ap()
    side = nc.alloc_psum_tensor("side", [P, 2, 1024], F32).ap()

    sem = nc.alloc_semaphore
    w_landed = [sem(f"w_landed{s}") for s in range(RING)]
    w_hi_done, w_lo_done = sem("w_hi_done"), sem("w_lo_done")
    first_loaded = sem("first_loaded")
    const_loaded, const_ready, halo_zeroed = sem("const_loaded"), sem("const_ready"), sem("halo_zeroed")
    acc_done = sem("acc_done")
    acc_free = [sem(f"acc_free{s}") for s in range(2)]
    side_done, side_free = sem("side_done"), sem("side_free")
    z_sig_ready, sig_used = sem("z_sig_ready"), sem("sig_used")
    cpy_used, ext_used = sem("cpy_used"), sem("ext_used")
    vn_ready, pooled_ready, sums_ready = sem("vn_ready"), sem("pooled_ready"), sem("sums_ready")
    res_ready, merge_ready = sem("res_ready"), sem("merge_ready")
    xs_ready, h_hi_done, h_ready = sem("xs_ready"), sem("h_hi_done"), sem("h_ready")
    h_odd_ready, y_scaled, y_odd_ready = sem("h_odd_ready"), sem("y_scaled"), sem("y_odd_ready")
    sq_ready, sumsq_ready, diag_ready = sem("sq_ready"), sem("sumsq_ready"), sem("diag_ready")
    msq_ready, rstd_ready = sem("msq_ready"), sem("rstd_ready")
    ln_ready, lnsig_ready = sem("ln_ready"), sem("lnsig_ready")
    x_loaded = [sem(f"x_loaded{b}") for b in range(KT // 2)]
    xres_loaded, y_ready, y_stored = sem("xres_loaded"), sem("y_ready"), sem("y_stored")
    states_ready, states_stored, v_stored = sem("states_ready"), sem("states_stored"), sem("v_stored")

    def width(j):
        return WMAX if j == NBLK - 1 else BLK

    def tiles(j):
        return [(0, WMAX // 2), (WMAX // 2, WMAX // 2)] if j == NBLK - 1 else [(0, BLK)]

    def n_tok(j):
        return BLK // P + (1 if j == NBLK - 1 else 0)

    def rows_of(t):
        return DEC if t == BLK // P else P

    def accv(s, j):
        if j == NBLK - 1:
            return acc[:, s, :, 0:WMAX // 2]
        return acc[:, s, 0, :]

    def tv(ap, j):
        if j == NBLK - 1:
            return ap[:, 0:WMAX].rearrange("p (a b) -> p a b", a=2)
        return ap[:, 0:BLK]

    def segments(j, hist):
        s = [(0, BLK, hist)]
        return s + [(BLK, DEC, BLK + 2 * hist)] if j == NBLK - 1 else s

    def pieces(j, hist):
        out = []
        for t0, n, c0 in segments(j, hist):
            for b, (a0, m) in enumerate(tiles(j)):
                lo, hi = max(t0, a0), min(t0 + n, a0 + m)
                if lo < hi:
                    out.append((lo, hi - lo, c0 + lo - t0, b, lo - a0))
        return out

    def side_pieces(j):
        return [(0, BLK), (BLK, DEC)] if j == NBLK - 1 else [(0, BLK)]

    def c1(name, i=0):
        return col[:, bass.ds(COLS[name] + i, 1)]

    def f(ap):
        return ap.bitcast(F32)

    TPB = BLK // P

    def h_count(j, k):
        return k // 2 if j == 0 else KT // 2 + (j - 1) * KT + k

    Y_GROUPS = [(0, 3), (3, 6), (6, KT)]

    def load_x(eng, j):
        for b in range(KT // 2):
            eng.dma_start(xr[:, 2 * b:2 * b + 2, 0:width(j)],
                          x_t[:, 2 * b:2 * b + 2, j * BLK:j * BLK + width(j)]).then_inc(x_loaded[b], 16)

    def each(eng, start, end, body):
        if end - start == 1:
            body(start)
        else:
            with eng.Fori(start, end) as i:
                body(i)

    block = nc.Block()
    blk = block.__enter__()

    @blk.sync
    def _(sp):
        def load(u, r, src, n):
            if not isinstance(u, int) or u >= RING:
                sp.wait_ge(w_lo_done, u - RING + 1)
            sp.dma_start(w_raw[r % RING][:, 0:n], src).then_inc(w_landed[r % RING], 16)

        load_x(sp, 0)
        for b in range(KT // 2 - 1):
            sp.wait_ge(x_loaded[b], 16)
        for j in range(NBLK):
            for name, count in SECTIONS:
                u0 = j * UPB + UNIT0[name]
                if name[0] == "G":
                    ph = int(name[1])

                    def body(i):
                        for r in range(4):
                            m = i * 2 + r // 2
                            if r % 2 == 0:
                                src = w_main[bass.ds(MAIN0[name] + m, 1), :, :].rearrange("o p n -> (o p) n")
                                load(u0 + i * 4 + r, r, src, DM)
                            else:
                                src = w_branch[bass.ds(ph * KT + m, 1), :, :].rearrange("o p n -> (o p) n")
                                load(u0 + i * 4 + r, r, src, WB)
                    each(sp, 0, count // 4, body)
                else:
                    def body(i):
                        for r in range(4):
                            src = w_main[bass.ds(MAIN0[name] + i * 4 + r, 1), :, :].rearrange("o p n -> (o p) n")
                            load(u0 + i * 4 + r, r, src, DM)
                    if j == 0 and name == "B":
                        body(0)
                        body(1)
                    else:
                        each(sp, 0, count // 4, body)

    @blk.gpsimd
    def _(pool):
        def lo(u, r, n):
            pool.wait_ge(w_hi_done, u + 1)
            s = r % RING
            pool.tensor_tensor(w_lo[s][:, 0:n], w_raw[s][:, 0:n], f(w_hi[s])[:, 0:n],
                               ALU.subtract).then_inc(w_lo_done, 1)

        def tick(u, r, like):
            if not isinstance(u, int) or u + AHEAD < NU:
                lo(u + AHEAD, r + AHEAD, unit_tiles(like + AHEAD) * P)

        powers = [0]

        def power(n, rows=P):
            powers[0] += 1
            pool.wait_ge(msq_ready, powers[0])
            pool.tensor_tensor(rstd[0:rows, 0:n], msq[0:rows, 0:n], nhalf[0:rows, 0:n],
                               ALU.pow).then_inc(rstd_ready, 1)

        pool.memset(nhalf[:, :], -0.5)
        pool.memset(halo_g[:, :, :], 0.0)
        pool.memset(halo_c[:, :, :], 0.0)
        pool.memset(halo_d[:, :, :], 0.0)
        pool.drain().then_inc(halo_zeroed, 1)
        pool.wait_ge(halo_zeroed, 1)
        def h_part(j, k):
            pool.wait_ge(h_hi_done, j * KT + k + 1)
            w = width(j)
            pool.tensor_tensor(h_lo[:, k, 0:w], xr[:, k, 0:w], f(h_hi)[:, k, 0:w], ALU.subtract).then_inc(h_ready, 1)

        power(TPB + 1)
        lo(0, 0, DM)
        for k in range(0, KT, 2):
            h_part(0, k)
            if k == 2:
                lo(1, 1, DM)
        lo(2, 2, DM)
        for j in range(NBLK):
            last = j == NBLK - 1
            for name, count in SECTIONS:
                u0 = j * UPB + UNIT0[name]

                def body(i, like=0):
                    for r in range(4):
                        tick(u0 + i * 4 + r, r, u0 + like * 4 + r)
                n = count // 4
                if name in ("B", "O"):
                    for r in range(count):
                        tick(u0 + r, r, u0 + r)
                        if name == "B" and j and r == 1:
                            power(TPB + 1)
                        if name == "O" and not last:
                            h_part(j + 1, r)
                elif n == 1:
                    body(0)
                else:
                    first = int(name == "G3" and not last)
                    if first:
                        body(0)
                        power(TPB + 1)
                    each(pool, first, n - 1, body)
                    if name == "G1":
                        power(TPB + 1)
                    body(n - 1, n - 1)
                if name == "V":
                    power(n=TPB)
                    if last:
                        power(1, DEC)
        power(TPB + 1)
        pool.wait_ge(xres_loaded, 16 * NBLK)
        for m in range(1, KT, 2):
            pool.wait_ge(y_scaled, m // 2 + 1)
            pool.tensor_tensor(xr[:, m, :], xr[:, m, :], yT[:, m, :], ALU.add).then_inc(y_odd_ready, 1)

    @blk.scalar
    def _(act):
        def hi(u, r, n):
            s = r % RING
            act.wait_ge(w_landed[s], (u // RING + 1) * 16)
            act.activation(w_hi[s][:, 0:n], w_raw[s][:, 0:n], ACT.Copy).then_inc(w_hi_done, 1)

        def tick(u, r, like):
            if isinstance(u, int) and u + AHEAD >= NU:
                return
            s = (r + AHEAD) % RING
            n = unit_tiles(like + AHEAD) * P
            if not isinstance(u, int) or u >= 1:
                act.wait_ge(acc_done, u)
            act.wait_ge(w_landed[s], (u - r) * (16 // RING) + ((r + AHEAD) // RING + 1) * 16)
            act.activation(w_hi[s][:, 0:n], w_raw[s][:, 0:n], ACT.Copy).then_inc(w_hi_done, 1)

        def done(u):
            act.wait_ge(acc_done, u + 1)

        def sigmoid(j, u, r, q, par, ready, bias=0.0):
            done(u)
            if not isinstance(q, int) or q >= 2:
                act.wait_ge(sig_used, q - 1)
            act.activation(tv(sig[par], j), accv(r % 2, j), ACT.Sigmoid, bias=bias).then_inc(ready, 1)

        def load_xres(j):
            act.dma_start(xr[:, :, 0:width(j)], x_t[:, :, j * BLK:j * BLK + width(j)]).then_inc(xres_loaded, 16)

        def store_y(j, g):
            a, b = Y_GROUPS[g]
            act.wait_ge(y_ready, j * KT + b)
            act.dma_start(y_t[:, a:b, j * BLK:j * BLK + width(j)], xr[:, a:b, 0:width(j)]).then_inc(y_stored, 16)

        def h_part(j, k):
            act.wait_ge(xs_ready, j * KT + k + 1)
            w = width(j)
            act.activation(h_hi[:, k, 0:w], xr[:, k, 0:w], ACT.Copy).then_inc(h_hi_done, 1)

        for dst, src in [(ident[:, :], ident_in), (col[:, :], cols)]:
            act.dma_start(dst, src).then_inc(first_loaded, 16)
        act.wait_ge(halo_zeroed, 1)
        act.activation(halo_g[:, 0, :], halo_g[:, 0, :], ACT.Square)
        for k in range(KT):
            act.wait_ge(x_loaded[k // 2], 16)
            if k >= 2:
                act.wait_ge(sig_used, k - 1)
            act.activation(sig[k % 2][:, 0:BLK], xr[:, k, 0:BLK], ACT.Square).then_inc(sq_ready, 1)
        for dst, src in [(bs_bc[:, :, :], bs_rows.partition_broadcast(P)),
                         (ws[:, :, :], ws_t), (tmp[:, 0:P], mask_t), (poolw[:, :, :], pool_w),
                         (smp_g[:, :, :], st_conv), (smp_c[:, :, :], st_pool), (smp_d[:, :, :], st_short),
                         (lnv_g_bc[:, :], rows[0:WB].partition_broadcast(P)),
                         (lnv_b_bc[:, :], rows[WB:2 * WB].partition_broadcast(P))]:
            act.dma_start(dst, src).then_inc(const_loaded, 16)
        hi(0, 0, DM)
        hi(1, 1, DM)
        for k in range(KT):
            h_part(0, k)
        hi(2, 2, DM)

        for j in range(NBLK):
            last = j == NBLK - 1
            ub = j * UPB
            q0 = KT + j * 64
            u0 = ub + UNIT0["B"]
            for r in range(8):
                u = u0 + r
                tick(u, r, u)
                if r % 2 == 0:
                    sigmoid(j, u, r, q0 + r // 2, (r // 2) % 2, acc_free[r % 2])
                if j and r == 0:
                    act.wait_ge(h_ready, h_count(j, KT))
                    load_xres(j - 1)
                if j and r in (5, 7):
                    store_y(j - 1, (r - 5) // 2)
            u0 = ub + UNIT0["V"]
            for r in range(4):
                tick(u0 + r, r, u0 + r)
                if j and r == 0:
                    store_y(j - 1, 2)
                done(u0 + r)
                act.activation(tv(vT[:, r, :], j), accv(r % 2, j), ACT.Copy).then_inc(acc_free[r % 2], 1)
            u0 = ub + UNIT0["C"]
            for r in range(8):
                u = u0 + r
                tick(u, r, u)
                c = r // 4 * 2 + r % 2
                if r % 4 < 2:
                    done(u)
                    if j * CT + c >= 2:
                        act.wait_ge(ext_used, j * CT + c - 1)
                    pcs = pieces(j, PH)
                    for n, (t0, m, c0, b, a0) in enumerate(pcs):
                        ins = act.activation(ext[c % 2][:, c0:c0 + m], acc[:, r % 2, b, a0:a0 + m], ACT.Copy)
                    ins.then_inc(acc_free[r % 2], 1)
                else:
                    sigmoid(j, u, r, q0 + 4 + c, c % 2, z_sig_ready)
            u0 = ub + UNIT0["M"]
            for r in range(8):
                u = u0 + r
                c = r // 2
                tick(u, r, u)
                if r % 2 == 0:
                    done(u)
                    if j * 8 + c >= 2:
                        act.wait_ge(cpy_used, j * 8 + c - 1)
                    act.activation(tv(cpy[c % 2], j), accv(0, j), ACT.Copy).then_inc(acc_free[0], 1)
                else:
                    sigmoid(j, u, r, q0 + 8 + c, c % 2, z_sig_ready)
                if last and r == 1:
                    act.wait_ge(vn_ready, j + 1)
                    act.dma_start(v_s, v_n[0:DEC, TPB, :]).then_inc(v_stored, 16)

            def gates(ph, qg):
                u0 = ub + UNIT0[f"G{ph}"]

                def body(i, like=0):
                    for r in range(4):
                        tick(u0 + i * 4 + r, r, u0 + like * 4 + r)
                        if r % 2 == 0:
                            m = i * 2 + r // 2
                            sigmoid(j, u0 + i * 4 + r, r, q0 + qg + m, (r // 2) % 2, acc_free[0],
                                    c1("b_gate", BRANCHES[ph] * KT + m))
                each(act, 0, 3, body)
                body(3, 3)

            gates(0, 12)
            u0 = ub + UNIT0["D"]

            def body_d(i, par, like):
                for r in range(4):
                    u = u0 + i * 4 + r
                    tick(u, r, u0 + like * 4 + r)
                    if r == 0:
                        done(u)
                        act.wait_ge(cpy_used, i + (j * 8 + 4 - 1))
                        act.activation(tv(cpy[par], j), accv(0, j), ACT.Copy).then_inc(acc_free[0], 1)
                    if r == 3:
                        sigmoid(j, u, r, q0 + 20 + i, par, z_sig_ready)
            for i in range(4):
                body_d(i, i % 2, i)
            gates(1, 24)
            u0 = ub + UNIT0["Z"]
            for r in range(4):
                tick(u0 + r, r, u0 + r)
                act.wait_ge(ln_ready, j * CT + r + 1)
                act.wait_ge(sig_used, q0 + 32 + 2 * r - 1)
                act.activation(sig[0][:, 0:width(j)], cb[:, r, 0:width(j)], ACT.Sigmoid,
                               bias=c1("ln_b", r), scale=c1("ln_g", r)).then_inc(lnsig_ready, 1)
                sigmoid(j, u0 + r, r, q0 + 32 + 2 * r + 1, 1, z_sig_ready)
            if not last:
                load_x(act, j + 1)
            gates(2, 40)
            gates(3, 48)
            u0 = ub + UNIT0["O"]
            for r in range(8):
                u = u0 + r
                tick(u, r, u)
                done(u)
                act.wait_ge(sig_used, q0 + 56 + r - 1)
                act.activation(tv(sig[r % 2], j), accv(r % 2, j), ACT.Square).then_inc(sq_ready, 1)
                act.activation(tv(yT[:, r, :], j), accv(r % 2, j), ACT.Copy,
                               scale=c1("g_post", r)).then_inc(acc_free[r % 2], 1)
                if not last:
                    h_part(j + 1, r)
                elif r == 0:
                    act.wait_ge(v_stored, 16)
                    load_xres(j)
        j = NBLK - 1
        for m in range(0, KT, 2):
            act.wait_ge(y_ready, j * KT + m // 2 + 1)
            act.wait_ge(y_odd_ready, m // 2 + 1)
            act.dma_start(y_t[:, m:m + 2, j * BLK:j * BLK + width(j)],
                          xr[:, m:m + 2, 0:width(j)]).then_inc(y_stored, 16)
        act.wait_ge(states_ready, 1)
        for dst, src in [(conv_p, halo_g), (pool_p, halo_c), (short_p, halo_d),
                         (conv_s, smp_g), (pool_s, smp_c), (short_s, smp_d)]:
            act.dma_start(dst, src[:, :, :]).then_inc(states_stored, 16)
        act.wait_ge(states_stored, 16 * 6)
        act.wait_ge(y_stored, 16 * (len(Y_GROUPS) * (NBLK - 1) + KT // 2))

    @blk.vector
    def _(dve):
        msqs = [0]

        def rstd_rows(j, k):
            dve.wait_ge(side_done, k + 1)
            dve.drain()
            ins = dve.tensor_scalar(msq[:, 0:TPB], side[:, k % 2, 0:TPB], EPS, None, ALU.add)
            if j == NBLK - 1:
                ins = dve.tensor_scalar(msq[0:DEC, TPB:TPB + 1], side[0:DEC, k % 2, TPB:TPB + 1], EPS, None, ALU.add)
            ins.then_inc(msq_ready, 1)
            msqs[0] += 1
            dve.drain().then_inc(side_free, 1)
            dve.wait_ge(rstd_ready, msqs[0])
            n = n_tok(j)
            dve.tensor_tensor(diag[:, 0:n, :], ident[:, :].unsqueeze(1).to_broadcast([P, n, P]),
                              rstd[:, 0:n].unsqueeze(2).to_broadcast([P, n, P]), ALU.mult).then_inc(diag_ready, 1)

        def add_square(dst, sq, w, first):
            if first:
                dve.tensor_copy(dst[:, 0:w], sq[:, 0:w])
            else:
                dve.tensor_tensor(dst[:, 0:w], dst[:, 0:w], sq[:, 0:w], ALU.add)

        def x_scaled(j, k, job):
            w = width(j)
            dve.scalar_tensor_tensor(xr[:, k, 0:w], xr[:, k, 0:w], c1("g_pre", k), side[:, job % 2, 0:w],
                                     ALU.mult, ALU.mult).then_inc(xs_ready, 1)

        def y_chunk(j, m, job):
            w = width(j)
            dve.tensor_tensor(yT[:, m, 0:w], yT[:, m, 0:w], side[:, job % 2, 0:w], ALU.mult)
            dve.drain()
            dve.tensor_tensor(xr[:, m, 0:w], xr[:, m, 0:w], yT[:, m, 0:w], ALU.add).then_inc(y_ready, 1)

        def ready_at(s, half):
            dve.wait_ge(acc_free[s], half + 1)

        def result(j, buf, c, semaphore=None, before=None):
            w = width(j)
            hi = out_hi[buf][:, bass.ds(c, 1), 0:w].rearrange("p o w -> p (o w)")
            lo = out_lo[buf][:, bass.ds(c, 1), 0:w].rearrange("p o w -> p (o w)")
            dve.tensor_copy(hi, tmp[:, 0:w])
            if before is not None:
                dve.drain().then_inc(before, 1)
            else:
                dve.drain()
            dve.tensor_tensor(lo, tmp[:, 0:w], f(hi), ALU.subtract).then_inc(res_ready, 1)

        def conv_step(j, t):
            dve.drain()
            for c in range(CT):
                for t0, n, c0 in segments(j, CH):
                    src = glu[:, c, bass.ds(c0 - CH + t, n)]
                    dst = cb[:, c, t0:t0 + n]
                    if isinstance(t, int) and t == 0:
                        dve.tensor_scalar(dst, src, c1("conv_w", c * CK), c1("conv_bias", c), ALU.mult, ALU.add)
                    else:
                        dve.scalar_tensor_tensor(dst, src, c1("conv_w", c * CK + t), dst, ALU.mult, ALU.add)

        dve.memset(mean_mat[:, :], 1.0 / WB)
        dve.memset(mean_dm[:, :], 1.0 / DM)
        dve.memset(ones[:, :], 1.0)
        dve.memset(msq[:, :], 1.0)
        for k in range(KT):
            dve.wait_ge(sq_ready, k + 1)
            dve.drain()
            add_square(sq_x, sig[k % 2], BLK, k == 0)
            dve.drain().then_inc(sig_used, 1)
        dve.drain().then_inc(sumsq_ready, 1)
        dve.wait_ge(first_loaded, 32)
        rstd_rows(0, SIDE["H", 0])
        dve.wait_ge(side_done, SIDE["H", 0] + 2)
        for k in range(KT):
            x_scaled(0, k, SIDE["H", 0] + 1)
            if k % 2:
                dve.drain()
                dve.wait_ge(h_hi_done, k + 1)
                dve.tensor_tensor(h_lo[:, k, 0:BLK], xr[:, k, 0:BLK], f(h_hi)[:, k, 0:BLK],
                                  ALU.subtract).then_inc(h_odd_ready, 1)
        dve.drain().then_inc(side_free, 1)
        dve.wait_ge(const_loaded, 16 * 9)
        dve.tensor_tensor(ws[:, :, :], ws[:, :, :], tmp[:, 0:P].unsqueeze(1).to_broadcast([P, CT, P]), ALU.mult)
        dve.wait_ge(halo_zeroed, 1)
        dve.drain().then_inc(const_ready, 1)

        for j in range(NBLK):
            last = j == NBLK - 1
            ub = j * UPB
            w = width(j)
            dve.wait_ge(acc_done, ub + 2)
            dve.drain()
            dve.tensor_copy(glu[:, :, 0:CH], halo_g[:, :, :])
            if last:
                dve.tensor_copy(glu[:, :, CH + BLK:2 * CH + BLK], smp_g[:, :, :])
            for c in range(CT):
                u = ub + UNIT0["B"] + 2 * c
                ready_at(0, u // 2)
                dve.wait_ge(acc_done, u + 2)
                for t0, m, c0, b, a0 in pieces(j, CH):
                    ins = dve.tensor_tensor(glu[:, c, c0:c0 + m], acc[:, 1, b, a0:a0 + m],
                                            sig[c % 2][:, t0:t0 + m], ALU.mult)
                ins.then_inc(acc_free[1], 1)
                dve.drain().then_inc(sig_used, 1)
                if j:
                    k = SIDE["Y", j]
                    if c == 0:
                        rstd_rows(j - 1, k)
                    else:
                        if c == 1:
                            dve.wait_ge(xres_loaded, 16 * j)
                            dve.wait_ge(side_done, k + 2)
                        for m in range(*Y_GROUPS[c - 1]):
                            y_chunk(j - 1, m, k + 1)
                        if c == 3:
                            dve.drain().then_inc(side_free, 1)
            dve.drain()
            dve.tensor_copy(halo_g[:, :, :], glu[:, :, BLK:BLK + CH])
            if last:
                dve.tensor_copy(smp_g[:, :, :], glu[:, :, CH + BLK + DEC:2 * CH + BLK + DEC])
            for t in range(3):
                conv_step(j, t)
            k = SIDE["V", j]
            dve.wait_ge(side_done, k + 2)

            def v_tile(t):
                if t == TPB:
                    return side[0:DEC, (k + 2) % 2, 0:WB]
                return side[:, (k + t // 2) % 2, t % 2 * 512:t % 2 * 512 + WB]

            for t in range(TPB):
                dve.bn_stats(stats[:, t, :], v_tile(t))
            dve.drain()
            for t in range(TPB):
                dve.bn_aggr(mv[:, t, :], stats[:, t, :])
            dve.drain()
            dve.tensor_scalar(msq[:, 0:TPB], mv[:, 0:TPB, 1], EPS, None, ALU.add).then_inc(msq_ready, 1)
            msqs[0] += 1
            dve.wait_ge(rstd_ready, msqs[0])
            if j:
                dve.wait_ge(y_stored, 16 * len(Y_GROUPS) * j)

            def v_norm(t, n, r):
                dve.tensor_scalar(v_n[0:n, t, :], v_tile(t), mv[0:n, t, 0:1], rstd[0:n, r:r + 1],
                                  ALU.subtract, ALU.mult)

            def v_affine(t, n):
                dve.tensor_tensor(v_n[0:n, t, :], v_n[0:n, t, :], lnv_g_bc[0:n, :], ALU.mult)
                dve.drain()
                dve.tensor_tensor(v_n[0:n, t, :], v_n[0:n, t, :], lnv_b_bc[0:n, :], ALU.add)

            for t in range(TPB):
                v_norm(t, P, t)
                if t % 2:
                    dve.drain().then_inc(side_free, 1)
            for t in range(TPB):
                v_affine(t, P)
            if last:
                dve.wait_ge(side_done, k + 3)
                dve.bn_stats(stats[0:DEC, TPB, :], v_tile(TPB))
                dve.drain()
                dve.bn_aggr(mv[0:DEC, TPB, :], stats[0:DEC, TPB, :])
                dve.drain()
                dve.tensor_scalar(msq[0:DEC, 0:1], mv[0:DEC, TPB, 1:2], EPS, None, ALU.add).then_inc(msq_ready, 1)
                msqs[0] += 1
                dve.wait_ge(rstd_ready, msqs[0])
                v_norm(TPB, DEC, 0)
                dve.drain().then_inc(side_free, 1)
                v_affine(TPB, DEC)
            dve.drain().then_inc(vn_ready, 1)

            def pool_chunk(c):
                e = ext[c % 2]
                length = BLK + PH + (PH + DEC if last else 0)
                ready_at(c % 2, (ub + UNIT0["C"]) // 2 + c // 2 * 2)
                src, bufs = e, [win_a, win_b]
                for s in range(c + 1):
                    d = 1 << s
                    lo = 2 * d - 1
                    dst = bufs[s % 2]
                    dve.tensor_tensor(dst[:, lo:length], src[:, lo:length], src[:, lo - d:length - d], ALU.add)
                    dve.drain()
                    src = dst
                win = 2 << c
                ps = pooled[c % 2]
                for t0, n, c0 in segments(j, PH):
                    dve.scalar_tensor_tensor(ps[:, t0:t0 + n], src[:, c0:c0 + n], 1.0 / win, e[:, c0:c0 + n],
                                             ALU.mult, ALU.subtract)
                if j == 0:
                    dve.drain()
                    m = win - 1
                    iv = COLS["inv_count"]
                    dve.tensor_tensor(ps[:, 0:m], src[:, PH:PH + m], col[:, iv:iv + m], ALU.mult)
                    dve.drain()
                    dve.tensor_tensor(ps[:, 0:m], ps[:, 0:m], e[:, PH:PH + m], ALU.subtract)
                dve.drain().then_inc(pooled_ready, 1)
                dve.tensor_copy(halo_c[:, c, :], e[:, BLK:BLK + PH])
                if last:
                    dve.tensor_copy(smp_c[:, c, :], e[:, PH + BLK + DEC:2 * PH + BLK + DEC])
                dve.drain().then_inc(ext_used, 1)

            for i in range(2):
                for c in (2 * i, 2 * i + 1):
                    dve.tensor_copy(ext[c % 2][:, 0:PH], halo_c[:, c, :])
                    if last:
                        dve.tensor_copy(ext[c % 2][:, PH + BLK:2 * PH + BLK], smp_c[:, c, :])
                    dve.drain()
                    pool_chunk(c)
                for c in (2 * i, 2 * i + 1):
                    u = ub + UNIT0["C"] + 4 * i + 2 + c % 2
                    dve.wait_ge(z_sig_ready, j * 16 + c + 1)
                    dve.tensor_tensor(tv(sig[c % 2], j), accv(u % 2, j), tv(sig[c % 2], j),
                                      ALU.mult).then_inc(acc_free[u % 2], 1)
                    k = SIDE["P", j] + c
                    dve.wait_ge(side_done, k + 1)
                    dve.drain()
                    dve.scalar_tensor_tensor(tmp[:, 0:w], side[:, k % 2, 0:w], c1("pool_scale", c),
                                             sig[c % 2][:, 0:w], ALU.mult, ALU.mult)
                    dve.drain().then_inc(side_free, 1)
                    result(j, 0, c, before=sig_used)
                    conv_step(j, 3 + c)
            for c in range(CT):
                u = ub + UNIT0["M"] + 2 * c
                k = SIDE["M", j] + c
                dve.wait_ge(side_done, k + 1)
                dve.drain()
                dve.tensor_tensor(tmp[:, 0:BLK].rearrange("p (a t) -> p a t", t=P),
                                  side[:, k % 2, 0:BLK].rearrange("p (a t) -> p a t", t=P),
                                  bs_bc[:, c, :].unsqueeze(1).to_broadcast([P, TPB, P]), ALU.add)
                if last:
                    dve.tensor_tensor(tmp[:, BLK:WMAX], side[:, k % 2, BLK:WMAX], bs_bc[:, c, 0:DEC], ALU.add)
                dve.drain().then_inc(side_free, 1)
                ready_at(0, u // 2)
                dve.tensor_tensor(tmp[:, 0:w], tmp[:, 0:w], cpy[c % 2][:, 0:w], ALU.mult)
                dve.drain().then_inc(cpy_used, 1)
                dve.wait_ge(z_sig_ready, j * 16 + 4 + c + 1)
                dve.tensor_tensor(tv(sig[c % 2], j), accv(1, j), tv(sig[c % 2], j),
                                  ALU.mult).then_inc(acc_free[1], 1)
                dve.drain()
                dve.tensor_tensor(tmp[:, 0:w], tmp[:, 0:w], sig[c % 2][:, 0:w], ALU.mult)
                dve.drain().then_inc(sig_used, 1)
                result(j, 1, c)
                conv_step(j, 7 + c)

            wn = width(min(j + 1, NBLK - 1))

            def merge(ph, start, end, with_conv=False):
                u0 = ub + UNIT0[f"G{ph}"]

                def body(i):
                    for r in range(2):
                        m = i * 2 + r
                        half = i * 2 + (u0 // 2 + r)
                        ready_at(0, half)
                        dve.wait_ge(acc_done, i * 4 + (u0 + 2 * r + 2))
                        dst = merged[:, bass.ds(m, 1), 0:w].rearrange("p o w -> p (o w)")
                        if ph == 0:
                            dve.tensor_tensor(tv(dst, j), accv(1, j), tv(sig[r], j),
                                              ALU.mult).then_inc(acc_free[1], 1)
                            dve.drain().then_inc(sig_used, 1)
                        else:
                            dve.tensor_tensor(tv(tmp, j), accv(1, j), tv(sig[r], j),
                                              ALU.mult).then_inc(acc_free[1], 1)
                            dve.drain().then_inc(sig_used, 1)
                            dve.tensor_tensor(dst, dst, tmp[:, 0:w], ALU.add)
                            if ph == 3:
                                dve.drain()
                                split_merged(m)
                        if ph == 2 and not last:
                            if r == 0:
                                dve.wait_ge(x_loaded[i], 16 * (j + 2))
                            dve.drain()
                            dve.tensor_tensor(tmp[:, 0:wn], xr[:, m, 0:wn], xr[:, m, 0:wn], ALU.mult)
                            dve.drain()
                            add_square(sq_x, tmp, wn, m == 0)
                        if ph == 3 and not last and i >= 2:
                            for k in (2 * (m - CT), 2 * (m - CT) + 1):
                                x_scaled(j + 1, k, SIDE["H", j + 1] + 1)
                        if with_conv:
                            conv_step(j, m + 11)
                        dve.drain()
                dve.drain()
                if ph >= 2:
                    for i in range(start, end):
                        body(i)
                else:
                    each(dve, start, end, body)

            def split_merged(m):
                b, c = m // CT, m % CT
                src, hi, lo = merged[:, m, 0:w], merged_hi[b][:, c, 0:w], merged_lo[b][:, c, 0:w]
                dve.tensor_copy(hi, src)
                dve.drain()
                dve.tensor_tensor(lo, src, f(hi), ALU.subtract).then_inc(merge_ready, 1)

            merge(0, 0, 4, with_conv=True)

            def body_d(i, par):
                u = ub + UNIT0["D"]
                e = ext[0]
                dve.tensor_copy(e[:, 0:SH], halo_d[:, i, :])
                if last:
                    dve.tensor_copy(e[:, SH + BLK:2 * SH + BLK], smp_d[:, i, :])
                half = u // 2 + 2 * i
                ready_at(0, half)
                dve.wait_ge(acc_done, u + 4 * i + 2)
                for t0, m, c0, b, a0 in pieces(j, SH):
                    ins = dve.tensor_tensor(e[:, c0:c0 + m], acc[:, 1, b, a0:a0 + m], cpy[par][:, t0:t0 + m],
                                            ALU.mult)
                ins.then_inc(acc_free[1], 1)
                dve.drain().then_inc(cpy_used, 1)
                for tap in range(3):
                    for t0, m, c0 in segments(j, SH):
                        src, dst = e[:, c0 - SH + tap:c0 - SH + tap + m], tmp[:, t0:t0 + m]
                        if tap == 0:
                            dve.tensor_scalar(dst, src, c1("short_w", i * 3), None, ALU.mult)
                        else:
                            dve.scalar_tensor_tensor(dst, src, c1("short_w", i * 3 + tap), dst, ALU.mult, ALU.add)
                    dve.drain()
                dve.tensor_copy(halo_d[:, i, :], e[:, BLK:BLK + SH])
                if last:
                    dve.tensor_copy(smp_d[:, i, :], e[:, SH + BLK + DEC:2 * SH + BLK + DEC])
                conv_step(j, 19 + 3 * i)
                dve.wait_ge(acc_done, u + 4 * i + 3)
                dve.tensor_tensor(tv(tmp, j), accv(0, j), tv(tmp, j), ALU.mult).then_inc(acc_free[0], 1)
                conv_step(j, 20 + 3 * i)
                dve.wait_ge(z_sig_ready, j * 16 + 8 + i + 1)
                dve.tensor_tensor(tv(sig[par], j), accv(1, j), tv(sig[par], j),
                                  ALU.mult).then_inc(acc_free[1], 1)
                dve.drain()
                dve.tensor_tensor(tmp[:, 0:w], tmp[:, 0:w], sig[par][:, 0:w], ALU.mult)
                dve.drain().then_inc(sig_used, 1)
                result(j, 0, i)
                conv_step(j, 21 + 3 * i)
            for i in range(CT):
                body_d(i, i % 2)

            dve.drain()
            dve.tensor_tensor(win_b[:, 0:w], cb[:, 0, 0:w], cb[:, 1, 0:w], ALU.add)
            for c in (2, 3):
                dve.drain()
                ins = dve.tensor_tensor(win_b[:, 0:w], win_b[:, 0:w], cb[:, c, 0:w], ALU.add)
            ins.then_inc(sums_ready, 1)
            merge(1, 0, 1)
            k = SIDE["L", j]
            dve.wait_ge(side_done, k + 1)
            for c in range(CT):
                dve.tensor_tensor(cb[:, c, 0:w], cb[:, c, 0:w], side[:, k % 2, 0:w], ALU.subtract)
            dve.drain().then_inc(side_free, 1)
            dve.tensor_tensor(win_b[:, 0:w], cb[:, 0, 0:w], cb[:, 0, 0:w], ALU.mult)
            for c in (1, 2, 3):
                dve.tensor_tensor(tmp[:, 0:w], cb[:, c, 0:w], cb[:, c, 0:w], ALU.mult)
                dve.drain()
                ins = dve.tensor_tensor(win_b[:, 0:w], win_b[:, 0:w], tmp[:, 0:w], ALU.add)
                if c < 3:
                    dve.drain()
            ins.then_inc(sums_ready, 1)
            merge(1, 1, 3)
            rstd_rows(j, k + 1)
            merge(1, 3, 4)
            dve.wait_ge(side_done, k + 3)
            for c in range(CT):
                dve.tensor_tensor(cb[:, c, 0:w], cb[:, c, 0:w], side[:, (k + 2) % 2, 0:w],
                                  ALU.mult).then_inc(ln_ready, 1)
            dve.drain().then_inc(side_free, 1)
            for c in range(CT):
                u = ub + UNIT0["Z"] + c
                dve.wait_ge(lnsig_ready, j * CT + c + 1)
                dve.tensor_scalar(cb[:, c, 0:w], cb[:, c, 0:w], c1("ln_g", c), c1("ln_b", c), ALU.mult, ALU.add)
                dve.drain()
                dve.tensor_tensor(tmp[:, 0:w], cb[:, c, 0:w], sig[0][:, 0:w], ALU.mult)
                dve.drain().then_inc(sig_used, 1)
                dve.wait_ge(z_sig_ready, j * 16 + 12 + c + 1)
                dve.tensor_tensor(tv(sig[1], j), accv(u % 2, j), tv(sig[1], j), ALU.mult).then_inc(acc_free[u % 2], 1)
                dve.drain()
                dve.tensor_tensor(tmp[:, 0:w], tmp[:, 0:w], sig[1][:, 0:w], ALU.mult)
                dve.drain().then_inc(sig_used, 1)
                result(j, 1, c)
            dve.drain()
            merge(2, 0, 4)
            if not last:
                dve.drain().then_inc(sumsq_ready, 1)
            merge(3, 0, 1)
            if not last:
                rstd_rows(j + 1, SIDE["H", j + 1])
            merge(3, 1, 2)
            if not last:
                dve.wait_ge(side_done, SIDE["H", j + 1] + 2)
            merge(3, 2, 4)
            if not last:
                dve.drain().then_inc(side_free, 1)
            for m in range(KT):
                dve.wait_ge(sq_ready, KT * (j + 1) + m + 1)
                dve.drain()
                add_square(sq_y, sig[m % 2], w, m == 0)
                dve.drain().then_inc(sig_used, 1)
            dve.drain().then_inc(sumsq_ready, 1)
        dve.drain().then_inc(states_ready, 1)
        k = SIDE["Y", NBLK]
        rstd_rows(NBLK - 1, k)
        for s in range(2):
            dve.wait_ge(acc_free[s], NU // 2)
        dve.wait_ge(xres_loaded, 16 * NBLK)
        dve.wait_ge(side_done, k + 2)
        for m in range(0, KT, 2):
            dve.tensor_tensor(yT[:, m + 1, 0:WMAX], yT[:, m + 1, 0:WMAX], side[:, (k + 1) % 2, 0:WMAX],
                              ALU.mult).then_inc(y_scaled, 1)
            y_chunk(NBLK - 1, m, k + 1)

    @blk.tensor
    def _(pe):
        def run_unit(j, u, half, r, rhs_hi, rhs_lo, nk, per_k=None):
            s, slot = r % 2, r % RING
            if not isinstance(half, int) or half >= 1:
                pe.wait_ge(acc_free[s], half)
            pe.wait_ge(w_lo_done, u + 1)
            for k in range(nk):
                if per_k:
                    per_k(k)
                wk = slice(k * P, (k + 1) * P)
                for n, (wt, mv_) in enumerate([(w_hi, rhs_hi), (w_hi, rhs_lo), (w_lo, rhs_hi)]):
                    for b, (t0, m) in enumerate(tiles(j)):
                        ins = pe.matmul(acc[:, s, b, 0:m], wt[slot][:, wk], mv_[:, k, t0:t0 + m],
                                        start=(k == 0 and n == 0), stop=(k == nk - 1 and n == 2))
            ins.then_inc(acc_done, 1)

        def section(j, name, start, end, body):
            u0 = j * UPB + UNIT0[name]
            if j == 0 and name == "B":
                for i in range(start, end):
                    body(i, u0 + 4 * i, u0 // 2 + 2 * i)
            else:
                each(pe, start, end, lambda i: body(i, i * 4 + u0, i * 2 + u0 // 2))

        def full(j):
            return lambda i, u, half, r: run_unit(j, u + r, half + r // 2, r, h_hi, h_lo, KT)

        def slot_free(k):
            if not isinstance(k, int) or k >= 2:
                pe.wait_ge(side_free, k - 1)

        def sum_job(j, k, src, mean):
            slot_free(k)
            for t in range(n_tok(j)):
                n = rows_of(t)
                ins = pe.matmul(side[0:n, k % 2, t:t + 1], src[:, t * P:t * P + n], mean, start=True, stop=True)
            ins.then_inc(side_done, 1)

        diags = [0]

        def row_job(j, k):
            slot_free(k)
            diags[0] += 1
            pe.wait_ge(diag_ready, diags[0])
            for t in range(n_tok(j)):
                n = rows_of(t)
                ins = pe.matmul(side[:, k % 2, t * P:t * P + n], ones[0:n, :], diag[0:n, t, 0:n],
                                start=True, stop=True)
            ins.then_inc(side_done, 1)

        sumsqs = [0]

        def square_job(j, k, src):
            sumsqs[0] += 1
            pe.wait_ge(sumsq_ready, sumsqs[0])
            sum_job(j, k, src, mean_dm[:, 0:1])

        def h_wait(j, k):
            if j == 0 and k % 2:
                pe.wait_ge(h_odd_ready, k // 2 + 1)
            elif j == 0:
                pe.wait_ge(h_ready, k // 2 + 1)
            else:
                pe.wait_ge(h_ready, h_count(j, k + 1))

        square_job(0, SIDE["H", 0], sq_x)
        row_job(0, SIDE["H", 0] + 1)
        for j in range(NBLK):
            last = j == NBLK - 1
            w = width(j)
            ub = j * UPB
            for r in range(8):
                u = ub + r
                run_unit(j, u, u // 2, r, h_hi, h_lo, KT,
                         (lambda k: h_wait(j, k)) if r == 0 else None)
                if j and r == 1:
                    square_job(j - 1, SIDE["Y", j], sq_y)
                if j and r == 3:
                    row_job(j - 1, SIDE["Y", j] + 1)
            if j == 0:
                pe.wait_ge(const_ready, 1)
            u = ub + UNIT0["V"]
            for r in range(4):
                run_unit(j, u + r, (u + r) // 2, r, h_hi, h_lo, KT)
            k = SIDE["V", j]
            slot_free(k + 1)
            for c in range(CT):
                pe.wait_ge(acc_free[c % 2], (u + c) // 2 + 1)
                for t in range(TPB):
                    s = (k + t // 2) % 2
                    ins = pe.transpose(side[:, s, t % 2 * 512 + c * P:t % 2 * 512 + (c + 1) * P],
                                       vT[:, c, t * P:(t + 1) * P], ident[:, :])
                    if c == CT - 1 and t % 2:
                        ins.then_inc(side_done, 1)
            for i in range(2):
                for r in range(4):
                    u = ub + UNIT0["C"] + 4 * i + r
                    run_unit(j, u, u // 2, r, h_hi, h_lo, KT)
                    if last and i == 0 and r == 0:
                        k = SIDE["V", j] + 2
                        slot_free(k)
                        for c in range(CT):
                            ins = pe.transpose(side[0:DEC, k % 2, c * P:(c + 1) * P], vT[:, c, BLK:WMAX],
                                               ident[:, :])
                        ins.then_inc(side_done, 1)
                    if r >= 2:
                        c = 2 * i + r - 2
                        k = SIDE["P", j] + c
                        slot_free(k)
                        pe.wait_ge(pooled_ready, j * CT + c + 1)
                        for t0, m in side_pieces(j):
                            ins = pe.matmul(side[:, k % 2, t0:t0 + m], poolw[:, c, :], pooled[c % 2][:, t0:t0 + m],
                                            start=True, stop=True)
                        ins.then_inc(side_done, 1)
            for c in range(CT):
                u = ub + UNIT0["M"] + 2 * c
                run_unit(j, u, u // 2, u % RING, h_hi, h_lo, KT)
                k = SIDE["M", j] + c
                slot_free(k)
                pe.wait_ge(vn_ready, j + 1)
                for t in range(n_tok(j)):
                    n = rows_of(t)
                    ins = pe.matmul(side[:, k % 2, t * P:t * P + n], v_n[0:n, t, c * P:(c + 1) * P],
                                    ws[0:n, c, 0:n], start=True, stop=True)
                ins.then_inc(side_done, 1)
                run_unit(j, u + 1, u // 2, (u + 1) % RING, h_hi, h_lo, KT)

            def gated(ph, start, end):
                b = OUTBUF[ph]

                def body(i, u, half):
                    for r in (0, 2):
                        run_unit(j, u + r, half + r // 2, r, h_hi, h_lo, KT)
                        run_unit(j, u + r + 1, half + r // 2, r + 1, out_hi[b], out_lo[b], CT)
                if start == 0:
                    pe.wait_ge(res_ready, 16 * j + 4 * ph + 4)
                section(j, f"G{ph}", start, end, body)

            def l_job(k, n):
                slot_free(k)
                pe.wait_ge(sums_ready, n)
                for t0, m in side_pieces(j):
                    ins = pe.matmul(side[:, k % 2, t0:t0 + m], mean_mat[:, :], win_b[:, t0:t0 + m],
                                    start=True, stop=True)
                ins.then_inc(side_done, 1)

            def body4(i, u, half):
                for r in range(4):
                    run_unit(j, u + r, half + r // 2, r, h_hi, h_lo, KT)

            gated(0, 0, 4)
            section(j, "D", 0, 4, body4)
            gated(1, 0, 1)
            l_job(SIDE["L", j], 2 * j + 1)
            gated(1, 1, 3)
            pe.wait_ge(sums_ready, 2 * j + 2)
            sum_job(j, SIDE["L", j] + 1, win_b, mean_mat[:, 0:1])
            gated(1, 3, 4)
            row_job(j, SIDE["L", j] + 2)
            section(j, "Z", 0, 1, body4)
            gated(2, 0, 4)
            gated(3, 0, 1)
            if not last:
                square_job(j + 1, SIDE["H", j + 1], sq_x)
            gated(3, 1, 2)
            if not last:
                row_job(j + 1, SIDE["H", j + 1] + 1)
            gated(3, 2, 4)
            def rhs_k(parts, k):
                return parts[k // CT][:, k % CT, :]

            for m in range(KT):
                u = ub + UNIT0["O"] + m
                s, slot = m % 2, m % RING
                pe.wait_ge(acc_free[s], u // 2)
                pe.wait_ge(w_lo_done, u + 1)
                for k in range(KT):
                    if m == 0:
                        pe.wait_ge(merge_ready, j * KT + k + 1)
                    for n, (wt, parts) in enumerate([(w_hi, merged_hi), (w_hi, merged_lo), (w_lo, merged_hi)]):
                        for b, (t0, mm) in enumerate(tiles(j)):
                            ins = pe.matmul(acc[:, s, b, 0:mm], wt[slot][:, k * P:(k + 1) * P],
                                            rhs_k(parts, k)[:, t0:t0 + mm],
                                            start=(k == 0 and n == 0), stop=(k == KT - 1 and n == 2))
                ins.then_inc(acc_done, 1)
        square_job(NBLK - 1, SIDE["Y", NBLK], sq_y)
        row_job(NBLK - 1, SIDE["Y", NBLK] + 1)

    block.__exit__(None, None, None)


_OUTS = [("y_t", (P, KT, SEQ + DEC)), ("conv_p", (P, CT, CH)), ("pool_p", (P, CT, PH)),
         ("short_p", (P, CT, SH)), ("conv_s", (P, CT, CH)), ("pool_s", (P, CT, PH)), ("short_s", (P, CT, SH)),
         ("v_s", (DEC, WB))]


def kernel(x_prompt, x_sample, state_conformer_conv, state_pool, state_short_conv, g_pre, g_post, w_in,
           b_gate, ln_v_g, ln_v_b, w_s, b_s, conv_b_w, conv_b_bias, ln_b_g, ln_b_b, pool_w, pool_scale,
           conv_d_w, w_branch, w_out):
    import numpy as np
    import concourse.bacc as bacc
    from concourse.bass_utils import run_bass_kernel_spmd

    def tiles_of(w, c0):
        k = w.shape[0] // P
        return w[:, c0:c0 + P].reshape(k, P, P).transpose(1, 0, 2).reshape(P, k * P)

    w_in, w_br, w_o = (np.asarray(a)[0] for a in (w_in, w_branch, w_out))
    part = lambda p, c: tiles_of(w_in, p * WB + c * P)
    gate = lambda b, m: tiles_of(w_in, 12 * WB + b * DM + m * P)
    main = []
    for name, _ in SECTIONS:
        if name == "B":
            main += [part(p, c) for c in range(CT) for p in (B_B, B_A)]
        elif name == "V":
            main += [part(A_V, c) for c in range(CT)]
        elif name == "C":
            main += [part(p, 2 * i + c) for i in range(2) for p in (C_X, C_Z) for c in range(2)]
        elif name == "M":
            main += [part(p, c) for c in range(CT) for p in (A_U, A_Z)]
        elif name == "D":
            main += [part(p, c) for c in range(CT) for p in (D_C, D_X, D_B, D_Z)]
        elif name == "Z":
            main += [part(B_Z, c) for c in range(CT)]
        elif name == "O":
            main += [tiles_of(w_o, m * P) for m in range(KT)]
        else:
            main += [gate(BRANCHES[int(name[1])], m) for m in range(KT)]
    chan = lambda a: np.asarray(a).reshape(-1, P).T
    taps = lambda a: np.asarray(a)[0].reshape(-1, CT, P).transpose(2, 1, 0)
    inv_count = np.broadcast_to(1.0 / np.arange(1, 17, dtype=np.float32), (P, 16))
    cols = np.concatenate([chan(b_gate), taps(conv_b_w).reshape(P, -1), chan(conv_b_bias), chan(ln_b_g),
                           chan(ln_b_b), chan(pool_scale), taps(conv_d_w).reshape(P, -1), chan(g_pre),
                           chan(g_post), inv_count], axis=1)
    arrays = {
        "x_t": np.concatenate([np.asarray(x_prompt)[0], np.asarray(x_sample)[0]]).T.reshape(KT, P, -1)
                 .transpose(1, 0, 2),
        "w_main": np.stack(main),
        "w_branch": np.stack([tiles_of(w_br[b], m * P) for b in BRANCHES for m in range(KT)]),
        "cols": cols,
        "rows": np.concatenate([np.asarray(a).reshape(-1) for a in (ln_v_g, ln_v_b)]),
        "bs_rows": np.asarray(b_s)[0],
        "ws_t": np.asarray(w_s)[0].transpose(2, 0, 1),
        "mask_t": np.triu(np.ones((P, P), np.float32)),
        "pool_w": np.asarray(pool_w)[0].transpose(1, 0, 2),
        "ident": np.eye(P, dtype=np.float32),
        "st_conv": taps(state_conformer_conv[0]), "st_pool": taps(state_pool[0]),
        "st_short": taps(state_short_conv[0]),
    }
    nc = bacc.Bacc("TRN2", target_bir_lowering=False, num_devices=1)
    ins, args = {}, []
    for name, a in arrays.items():
        a = np.ascontiguousarray(a)
        ins[f"in_{name}"] = a
        args.append(nc.dram_tensor(f"in_{name}", a.shape, mybir.dt.from_np(a.dtype), kind="ExternalInput").ap())
    for name, shape in _OUTS:
        args.append(nc.dram_tensor(f"out_{name}", shape, F32, kind="ExternalOutput").ap())
    build(nc, *args)
    r = run_bass_kernel_spmd(nc, [ins], core_ids=[0]).results[0]
    got = {name: r[f"out_{name}"] for name, _ in _OUTS}
    rows_back = lambda a: a.transpose(2, 1, 0).reshape(1, 1, a.shape[2], WB)
    y = got["y_t"].transpose(2, 1, 0).reshape(1, SEQ + DEC, DM)
    return (y[:, :SEQ], y[:, SEQ:],
            rows_back(got["conv_p"]), rows_back(got["pool_p"]), rows_back(got["short_p"]),
            rows_back(got["conv_s"]), rows_back(got["pool_s"]), rows_back(got["short_s"]),
            got["v_s"].reshape(1, 1, DEC, WB))
```
